# Optimizing a Trainium2 kernel written in Bass

```python
import math
import jax, jax.numpy as jnp
from jax import lax
import numpy as np

D_MODEL = 1024
BATCH = 1
SEQ = 1024
DEPTH = 2

N_MEM = 256
HEAD_DIM = 64
N_DIL_HEADS = 12
DIL_WIDTH = N_DIL_HEADS * HEAD_DIM
DIL_PATTERNS = ((128, 1), (512, 4), (2048, 16))
BLOCK = 128
N_SGU_GROUPS = 12
SGU_GROUP_DIM = 64
SGU_WIDTH = N_SGU_GROUPS * SGU_GROUP_DIM
CHUNK = 128
N_MEM_HEADS = 4
MEM_WIDTH = N_MEM_HEADS * HEAD_DIM
MIX_WIDTH = DIL_WIDTH + MEM_WIDTH
D_FF = ((-(-8 * D_MODEL // 3) + 255) // 256) * 256
DN_ALPHA = (2 * DEPTH) ** 0.25
DN_BETA = (8 * DEPTH) ** -0.25
N_A = (DEPTH + 1) // 2
N_B = DEPTH // 2
IN_A = 3 * DIL_WIDTH + MEM_WIDTH
IN_B = 2 * SGU_WIDTH + MEM_WIDTH
LN_EPS = 1e-5

kernel_name = "hybrid_dilated_gmlp_memory_deepnorm"

def layer_norm(x, g, b):
    xf = x.astype(jnp.float32)
    mu = xf.mean(-1, keepdims=True)
    var = jnp.square(xf - mu).mean(-1, keepdims=True)
    y = (xf - mu) * lax.rsqrt(var + LN_EPS)
    return (y * g.astype(jnp.float32) + b.astype(jnp.float32)).astype(x.dtype)

def alibi_slopes(n):
    return jnp.exp2(-8.0 * (jnp.arange(n, dtype=jnp.float32) + 1.0) / n)

def band_pattern(q, k, v, slopes, window, dil):
    B, S, H, Dh = q.shape
    steps_max = window // dil
    L = S // dil
    n_blk = -(-L // BLOCK)
    Lp = n_blk * BLOCK
    def sub(t):
        return t.reshape(B, L, dil, H, Dh)
    qs = jnp.pad(sub(q), ((0, 0), (0, Lp - L), (0, 0), (0, 0), (0, 0)))
    qs = qs.reshape(B, n_blk, BLOCK, dil, H, Dh)
    def banded_keys(t):
        tp = jnp.pad(sub(t), ((0, 0), (BLOCK, Lp - L), (0, 0), (0, 0), (0, 0)))
        prev = tp[:, :Lp].reshape(B, n_blk, BLOCK, dil, H, Dh)
        cur = tp[:, BLOCK:].reshape(B, n_blk, BLOCK, dil, H, Dh)
        return jnp.concatenate([prev, cur], axis=2)
    kb = banded_keys(k)
    vb = banded_keys(v)
    s = jnp.einsum('bnqrhd,bnkrhd->bnrhqk', qs, kb).astype(jnp.float32) * (Dh ** -0.5)
    qi = jnp.arange(BLOCK)[:, None]
    ki = jnp.arange(2 * BLOCK)[None, :]
    steps = qi + BLOCK - ki
    key_idx = (jnp.arange(n_blk) * BLOCK)[:, None, None] - BLOCK + ki[None]
    valid = (steps >= 0) & (steps <= steps_max) & (key_idx >= 0)
    bias = -slopes[:, None, None] * (steps * dil).astype(jnp.float32)[None]
    s = s + bias[None, None, None]
    s = jnp.where(valid[None, :, None, None], s, -jnp.inf)
    m = s.max(-1, keepdims=True)
    p = jnp.exp(s - m)
    den = p.sum(-1)
    lse = m[..., 0] + jnp.log(den)
    o = jnp.einsum('bnrhqk,bnkrhd->bnqrhd', p.astype(v.dtype), vb)
    o = o / jnp.moveaxis(den, -1, 2)[..., None].astype(o.dtype)
    o = o.reshape(B, Lp, dil, H, Dh)[:, :L].reshape(B, S, H, Dh)
    lse = jnp.moveaxis(lse, -1, 2).reshape(B, Lp, dil, H)[:, :L].reshape(B, S, H)
    return o, lse

def dilated_attention(q, k, v):
    slopes = alibi_slopes(q.shape[2])
    outs, lses = [], []
    for window, dil in DIL_PATTERNS:
        o, lse = band_pattern(q, k, v, slopes, window, dil)
        outs.append(o)
        lses.append(lse)
    w = jax.nn.softmax(jnp.stack(lses, 0), axis=0).astype(q.dtype)
    return jnp.einsum('pbsh,pbshd->bshd', w, jnp.stack(outs, 0))

def causal_chunk_sgu(u, v, ln_g, ln_b, w_s, b_s):
    B, S, _ = v.shape
    v = layer_norm(v, ln_g, ln_b)
    vc = v.reshape(B, S // CHUNK, CHUNK, N_SGU_GROUPS, SGU_GROUP_DIM)
    ws = w_s * jnp.tril(jnp.ones((CHUNK, CHUNK), w_s.dtype))
    mixed = jnp.einsum('gts,bnsgc->bntgc', ws, vc) + b_s.T[None, None, :, :, None]
    return u * mixed.reshape(B, S, SGU_WIDTH)

def memory_attention(qm, mk, mv):
    s = jnp.einsum('bshd,bmhd->bhsm', qm, mk).astype(jnp.float32) * (HEAD_DIM ** -0.5)
    p = jax.nn.softmax(s, axis=-1).astype(mv.dtype)
    return jnp.einsum('bhsm,bmhd->bshd', p, mv)

def setup_inputs(seed: int = 0) -> dict:
    key = jax.random.key(seed)
    ks = jax.random.split(key, 18)
    f32 = jnp.float32
    D = D_MODEL
    def nrm(k, shape, scale):
        return jax.random.normal(k, shape, f32) * scale
    return {
        "x": nrm(ks[0], (BATCH, SEQ, D), 1.0),
        "mem": nrm(ks[1], (BATCH, N_MEM, D), 1.0),
        "a_w_in": nrm(ks[2], (N_A, D, IN_A), D ** -0.5),
        "b_w_in": nrm(ks[3], (N_B, D, IN_B), D ** -0.5),
        "sgu_ln_g": 1.0 + nrm(ks[4], (N_B, SGU_WIDTH), 0.02),
        "sgu_ln_b": nrm(ks[5], (N_B, SGU_WIDTH), 0.02),
        "sgu_w_s": nrm(ks[6], (N_B, N_SGU_GROUPS, CHUNK, CHUNK), CHUNK ** -0.5),
        "sgu_b_s": 1.0 + nrm(ks[7], (N_B, N_SGU_GROUPS, CHUNK), 0.02),
        "w_mem_kv": nrm(ks[8], (DEPTH, D, 2 * MEM_WIDTH), D ** -0.5),
        "w_out": nrm(ks[9], (DEPTH, MIX_WIDTH, D), DN_BETA * MIX_WIDTH ** -0.5),
        "ln_mix_g": 1.0 + nrm(ks[10], (DEPTH, D), 0.02),
        "ln_mix_b": nrm(ks[11], (DEPTH, D), 0.02),
        "w_gate": nrm(ks[12], (DEPTH, D, D_FF), D ** -0.5),
        "w_up": nrm(ks[13], (DEPTH, D, D_FF), D ** -0.5),
        "w_down": nrm(ks[14], (DEPTH, D_FF, D), DN_BETA * D_FF ** -0.5),
        "ln_ffn_g": 1.0 + nrm(ks[15], (DEPTH, D), 0.02),
        "ln_ffn_b": nrm(ks[16], (DEPTH, D), 0.02),
    }

def reference(x, mem, a_w_in, b_w_in, sgu_ln_g, sgu_ln_b, sgu_w_s, sgu_b_s, w_mem_kv, w_out,
              ln_mix_g, ln_mix_b, w_gate, w_up, w_down, ln_ffn_g, ln_ffn_b):
    B, S, _ = x.shape
    for i in range(DEPTH):
        j = i // 2
        mk, mv = jnp.split(mem @ w_mem_kv[i], 2, axis=-1)
        mk = mk.reshape(B, N_MEM, N_MEM_HEADS, HEAD_DIM)
        mv = mv.reshape(B, N_MEM, N_MEM_HEADS, HEAD_DIM)
        if i % 2 == 0:
            h = x @ a_w_in[j]
            q, k, v, qm = jnp.split(h, [DIL_WIDTH, 2 * DIL_WIDTH, 3 * DIL_WIDTH], axis=-1)
            hs = (B, S, N_DIL_HEADS, HEAD_DIM)
            mix = dilated_attention(q.reshape(hs), k.reshape(hs), v.reshape(hs)).reshape(B, S, DIL_WIDTH)
        else:
            h = x @ b_w_in[j]
            u, v, qm = jnp.split(h, [SGU_WIDTH, 2 * SGU_WIDTH], axis=-1)
            mix = causal_chunk_sgu(jax.nn.gelu(u), jax.nn.gelu(v), sgu_ln_g[j], sgu_ln_b[j],
                                   sgu_w_s[j], sgu_b_s[j])
        mo = memory_attention(qm.reshape(B, S, N_MEM_HEADS, HEAD_DIM), mk, mv).reshape(B, S, MEM_WIDTH)
        y = jnp.concatenate([mix, mo], axis=-1) @ w_out[i]
        x = layer_norm(DN_ALPHA * x + y, ln_mix_g[i], ln_mix_b[i])
        f = (jax.nn.silu(x @ w_gate[i]) * (x @ w_up[i])) @ w_down[i]
        x = layer_norm(DN_ALPHA * x + f, ln_ffn_g[i], ln_ffn_b[i])
    return x


_drawn_inputs = setup_inputs


def setup_inputs(seed=0):
    import zlib

    import numpy as np

    out = dict(_drawn_inputs(seed))
    spreads = {}
    factors = {}
    for name, (base, spread) in spreads.items():
        noise = np.random.default_rng([zlib.crc32(name.encode()), seed]).standard_normal(out[name].shape)
        drawn = base * np.exp(spread * noise) if base else spread * noise
        out[name] = __import__('jax').numpy.asarray(drawn.astype(out[name].dtype))
    for name, factor in factors.items():
        out[name] = (out[name] * factor).astype(out[name].dtype)
    return out
```

```python
import numpy as np
import concourse.bass as bass
import concourse.mybir as mybir

F32 = mybir.dt.float32
F32R = mybir.dt.float32r
I16 = mybir.dt.int16
ALU = mybir.AluOpType
ACT = mybir.ActivationFunctionType

P = 128
S = 1024
D = 1024
M = 256
HD = 64
NT = S // P
KT = D // P
DIL_W = 768
MEM_W = 256
NDP = DIL_W // P
NMP = MEM_W // P
FF = 2816
NG = DIL_W // HD
NCH = FF // (2 * P)
ALPHA = float((2 * 2) ** 0.25)
EPS = 1e-5
PATTERNS = ((128, 1), (512, 4), (2048, 16))
UNIT = 1024
WS = 6
RS = 2
QSCALE = HD ** -0.5

U_MEM = (0, 98)
U_DIL = 6
U_V, U_U = 104, 110
U_OUT = (24, 116)
U_FFN = (32, 124)
U_END = 190

KB = 1024
A_XTH, A_XTL, A_XR = 0, 32 * KB, 64 * KB
A_WH, A_WL, A_RAW = 96 * KB, 120 * KB, 144 * KB
A_MV, A_MO, A_X = 152 * KB, 176 * KB, 184 * KB
A_SMALL = 206 * KB


def tables():
    d = (np.arange(P)[:, None] - np.arange(S)[None, :] + (S - P)).astype(np.int64)
    count = np.zeros(d.shape, np.int64)
    for window, dil in PATTERNS:
        count += (d >= 0) & (d <= window) & (d % dil == 0)
    logc = np.where(count > 0, np.log(np.maximum(count, 1)), -1e30).astype(np.float32)
    slopes = np.exp2(-8.0 * (np.arange(NG) + 1.0) / NG).astype(np.float32)
    return ((-d).astype(np.int16), logc, np.tile(slopes, (P, 1)), np.eye(P, dtype=np.float32))


def build(nc, a, out):
    base = -(-nc.sbuf_base // 64) * 64

    def at(name, shape, dt, off):
        return nc.alloc_sbuf_tensor_at(name, shape, dt, offset=base + off)

    sems = {}

    def sem(name):
        if name not in sems:
            sems[name] = nc.alloc_semaphore(name)
        return sems[name]

    XTh = at("XTh", [P, KT, S], F32R, A_XTH)
    XTl = at("XTl", [P, KT, S], F32R, A_XTL)
    XR = at("XR", [P, NT, D], F32, A_XR)
    Wh = at("Wh", [P, WS, UNIT], F32R, A_WH)
    Wl = at("Wl", [P, WS, UNIT], F32R, A_WL)
    raw = at("raw", [P, RS, UNIT], F32, A_RAW)
    PTh = at("PTh", [P, NT, 2, P], F32R, A_WH + 12 * KB)
    Kh = at("Kh", [P, S], F32R, A_WH + 20 * KB)
    PTl = at("PTl", [P, NT, 2, P], F32R, A_WL + 12 * KB)
    Kl = at("Kl", [P, S], F32R, A_WL + 20 * KB)
    mixT = at("mixT", [P, NDP, S], F32, A_MV)
    MO = at("MO", [P, NMP, S], F32, A_MO)
    memTh = at("memTh", [P, KT, M], F32R, A_MV)
    memTl = at("memTl", [P, KT, M], F32R, A_MV + 8 * KB)
    memraw = at("memraw", [P, 2, D], F32, A_MV + 16 * KB)

    class MemBuf:
        Qh = at("mQh", [P, 2, S], F32R, A_X)
        Ql = at("mQl", [P, 2, S], F32R, A_X + 8 * KB)
        Vh = at("mVh", [P, 2, 192], F32R, A_MV + 16 * KB)
        Vl = at("mVl", [P, 2, 192], F32R, A_MV + 16 * KB + 1536)
        Pb = at("mP", [P, 2, M], F32, A_MV + 19 * KB)
        vT = at("mvT", [P, M], F32, A_MV + 21 * KB)
        RB = at("mRB", [P, 2, 2, HD], F32, A_X + 16 * KB)
        RSb = at("mRS", [P, 2 * P], F32, A_X + 17 * KB)
        zero = at("mzero", [P, M], F32, A_MV + 22 * KB)

    class DilBuf:
        Qh = at("dQh", [P, 2, S], F32R, A_XR)
        Ql = at("dQl", [P, 2, S], F32R, A_XR + 8 * KB)
        Vh = at("dVh", [P, NT, 192], F32R, A_XR + 16 * KB)
        Vl = at("dVl", [P, NT, 192], F32R, A_XR + 22 * KB)
        RB = at("dRB", [P, 2, 2, HD], F32, A_XR + 28 * KB)
        RSb = at("dRS", [P, 2 * P], F32, A_XR + 29 * KB)
        Pb = at("dP", [P, 2, S], F32, A_X)
        B = at("dB", [P, 2, S], F32, A_X + 8 * KB)
        vT = at("dvT", [P, S], F32, A_X)

    logc = at("logc", [P, S], F32, A_X + 16 * KB)
    ndist = at("ndist", [P, S], I16, A_X + 20 * KB)
    gb = at("gb", [P, 2, D], F32, A_X)
    hidh = at("hidh", [P, 2, S], F32R, A_MV)
    hidl = at("hidl", [P, 2, S], F32R, A_MV + 8 * KB)
    silu = at("silu", [P, 2, 512], F32, A_MO)
    hid = at("hid", [P, 2, 512], F32, A_MO + 4 * KB)
    V = at("V", [P, NT, DIL_W], F32, A_MV)
    WSh = at("WSh", [P, NG, P], F32R, A_X)
    WSl = at("WSl", [P, NG, P], F32R, A_X + 6 * KB)
    wsraw = at("wsraw", [P, NG, P], F32, A_X + 12 * KB)
    sgb = at("sgb", [P, 2, DIL_W], F32, A_X + 12 * KB)
    VSh = at("VSh", [P, 2, NT, HD], F32R, A_X + 12 * KB)
    VSl = at("VSl", [P, 2, NT, HD], F32R, A_X + 16 * KB)
    ub = at("ub", [P, 2, M], F32, A_X + 20 * KB)
    small_at = [A_SMALL]

    def small(name, shape):
        n = 4 * int(np.prod(shape[1:]))
        t = at(name, shape, F32, small_at[0])
        small_at[0] += -(-n // 32) * 32
        return t

    ident = small("ident", [P, P])
    slopes = small("slopes", [P, NG])
    mneg = small("mneg", [P, 16])
    den = small("den", [P, 16])
    rden = small("rden", [P, 16])
    st = small("st", [P, NT, 3, 6])
    mv = small("mv", [P, NT, 2])
    rstd = small("rstd", [P, NT])
    nmr = small("nmr", [P, NT])
    bst = small("bst", [P, NG])
    eps = small("eps", [P, 1])
    zcol = small("zcol", [P, 1])
    tick = small("tick", [P, 16])
    ps = nc.alloc_psum_tensor("ps", [P, 8 * 512], F32)

    def bank(b, n=512, off=0):
        return ps[:, 512 * b + off:512 * b + off + n]

    def cols(w, c0):
        return w[:, bass.ds(c0, P)].rearrange("(k p) c -> p k c", p=P)

    def load(sp, u, src):
        if not (isinstance(u, int) and u < RS):
            sp.wait_ge(split_done, u - RS + 1)
        slot = load.turn % RS
        load.turn += 1
        dst = raw[:, slot, :]
        if len(src.shape) == 3:
            dst = dst.rearrange("p (k c) -> p k c", c=P)
        sp.dma_start(dst, src).then_inc(raw_landed[slot], 16)

    load.turn = 0
    split_done = sem("split_done")
    raw_landed = [sem(f"raw_landed{i}") for i in range(RS)]

    def used(u, c=None):
        for L in range(2):
            v = u - U_MEM[L]
            if 0 <= v < 3 * NMP:
                return sem("mem_proj"), 4 * (v // 3 + NMP * L) + 2 + v % 3
            v = u - U_OUT[L]
            if 0 <= v < KT:
                return go[L]("product", 16 * (v // 2 + 1))
            v = u - U_FFN[L]
            if 0 <= v < 6 * NCH:
                c, j = (v // 6, v % 6) if c is None else (c, v)
                if j < 4:
                    return gf[L]("up", 4 * c + 3 + j // 2)
                return gf[L]("product", 16 * (c + 1))
        v = u - U_DIL
        if 0 <= v < 3 * NDP:
            return sem("dil_proj"), 6 * (v // 3) + 2 + 2 * (v % 3)
        return (sem("vproj_product"), 3 * NT) if u < U_U else (sem("uproj_product"), 3 * NT)

    def split(pool, u, slot, before=None, turn=None, rounds=None):
        turn = u % RS if turn is None else turn
        pool.wait_ge(raw_landed[turn], 16 * (u // RS + 1) if rounds is None else 16 * rounds)
        if before is not None:
            pool.wait_ge(*(before if isinstance(before, tuple) else used(before)))
        nc.gpsimd.tensor_tensor(Wh[:, slot, :], raw[:, turn, :], zcol[:, 0:1].to_broadcast([P, UNIT]),
                                ALU.add).then_inc(high_done, 1)
        pool.wait_ge(high_done, u + 1)
        nc.gpsimd.tensor_tensor(Wl[:, slot, :], raw[:, turn, :], Wh[:, slot, :].bitcast(F32),
                                ALU.subtract).then_inc(split_done, 1)

    high_done = sem("high_done")

    def three(dst, wh, wl, xh, xl, first, last):
        nc.tensor.matmul(dst, wh, xh, start=first, stop=False)
        nc.tensor.matmul(dst, wh, xl, start=False, stop=False)
        return nc.tensor.matmul(dst, wl, xh, start=False, stop=last)

    def wtile(slot, k):
        return Wh[:, slot, k * P:(k + 1) * P], Wl[:, slot, k * P:(k + 1) * P]

    def rows_in(dst, slot, xh, xl, lo, n):
        for k in range(KT):
            wh, wl = wtile(slot, k)
            mm = three(dst, wh, wl, xh[:, k, lo:lo + n], xl[:, k, lo:lo + n], k == 0, k == KT - 1)
        return mm

    def tile_of(n):
        return 2 * (n // 4) + n % 2, (n // 2) % 2

    def width(kind, n):
        return M if kind == "mem" else P * (tile_of(n)[0] + 1)

    def keytiles(kind, c):
        return 2 if kind == "mem" else 2 * c + 2

    def pair_names(kind):
        def g(name, value=None):
            s = sem(f"{kind}_{name}")
            return s if value is None else (s, value)
        return g

    def groups(kind):
        if kind == "mem":
            return [("q", 0, 0), ("q", 1, 1), ("k", 0, 2), ("v", 0, 4)]
        return [("q", 0, 0), ("q", 1, 1), ("k", 0, 2), ("k", 1, 3), ("v", 0, 4), ("v", 1, 5)]

    def s_view(kind, n, wide=False):
        w, b = width(kind, n), 2 * (n % 2)
        if w > 512:
            return ps[:, 512 * b:512 * b + 1024].rearrange("p (a c) -> p a c", c=512)[:, :, 0:w // 2]
        return bank(b, w)

    def pair_pe(pe, kind, L, pi, u, slots):
        g = pair_names(kind)
        bf = MemBuf if kind == "mem" else DilBuf
        Kn = M if kind == "mem" else S
        ng = len(groups(kind))
        pe.wait_ge(*g("mixed", pi * 4 + 1))
        seen = -1
        for j, (what, h, b) in enumerate(groups(kind)):
            un = "qkv".index(what)
            if un != seen:
                pe.wait_ge(split_done, u + un + 1)
                seen = un
            if what != "q" and kind == "mem":
                mm = rows_in(bank(b, M), slots[un], memTh, memTl, 0, M)
            else:
                mm = rows_in(bank(b), slots[un], XTh, XTl, h * 512, 512)
            mm.then_inc(g("proj"), 1)

        def scores(n):
            qt, hd = tile_of(n)
            w = width(kind, n)
            if n >= 2:
                pe.wait_ge(*g("logits", pi * 16 + n - 1))
            nb = max(256, w) if w <= 512 else w // 2
            for i in range(1 if w <= 512 else 2):
                dst = bank(2 * (n % 2) + i, nb)
                ks = slice(i * nb, (i + 1) * nb)
                q0 = slice(qt * P, (qt + 1) * P)
                mm = three(dst, bf.Qh[:, hd, q0], bf.Ql[:, hd, q0], Kh[:, ks], Kl[:, ks], True, True)
            mm.then_inc(g("scores"), 1)

        pe.wait_ge(*g("k_low", (pi + 1) * (Kn // min(Kn, 512))))
        pe.wait_ge(*g("q_low", (pi + 1) * 4))
        scores(0)
        scores(1)
        pe.wait_ge(*g("v_copied", (pi + 1) * (1 if kind == "mem" else 2)))
        for t in range(Kn // P):
            mm = nc.tensor.transpose(bank(6 + t // 4, P, (t % 4) * P), bf.vT[:, t * P:(t + 1) * P], ident[:, :])
            if t % 4 == 3 or t == Kn // P - 1:
                mm.then_inc(g("v_turned"), 1)
        nv = (Kn // P + 3) // 4
        for n in range(16):
            c, hd = n // 4, (n // 2) % 2
            pe.wait_ge(*g("probs", pi * 16 + n + 1))
            if n >= 1:
                pe.wait_ge(*g("pt_low", pi * 16 + n))
            for k in range(width(kind, n) // P):
                mm = nc.tensor.transpose(bank(4 + k // 4, P, (k % 4) * P),
                                         bf.Pb[:, n % 2, k * P:(k + 1) * P], ident[:, :])
            mm.then_inc(g("turned"), 1)
            if n + 2 < 16:
                scores(n + 2)
            if n % 2:
                s = n // 2
                pe.wait_ge(*g("pt_low", pi * 16 + n + 1))
                if s == 0:
                    pe.wait_ge(*g("v_low", (pi + 1) * nv))
                if kind == "dil":
                    pe.wait_ge(*g("pt_zero", (pi * 8 + s + 1) * 2))
                if hd == 0 and c >= 2:
                    pe.wait_ge(*g("mixed", pi * 4 + c))
                dst = bank(6 + c % 2, 2 * P)
                nk = keytiles(kind, c)
                for k in range(nk):
                    mm = three(dst, bf.Vh[:, k, HD * hd:HD * hd + P], bf.Vl[:, k, HD * hd:HD * hd + P],
                               PTh[:, k, :, :], PTl[:, k, :, :],
                               hd == 0 and k == 0, hd == 1 and k == nk - 1)
                mm.then_inc(g("pv"), 1)
                if hd == 1:
                    pe.wait_ge(*g("rden_wide", pi * 4 + c + 1))
                    for i in range(2):
                        mm = nc.tensor.transpose(bank(6 + c % 2, P, 256 + i * P),
                                                 bf.RB[:, i, :, :].rearrange("p a d -> p (a d)"), ident[:, :])
                    mm.then_inc(g("rden_turned"), 1)

    def pair_act(act, kind, L, pi):
        g = pair_names(kind)
        bf = MemBuf if kind == "mem" else DilBuf
        Kn = M if kind == "mem" else S
        ng = len(groups(kind))
        nv = (Kn // P + 3) // 4
        for j, (what, h, b) in enumerate(groups(kind)):
            act.wait_ge(*g("proj", pi * ng + j + 1))
            n = M if what != "q" and kind == "mem" else 512
            if what == "q":
                for hd in range(2):
                    r = slice(HD * hd, HD * hd + HD)
                    nc.scalar.activation(bf.Qh[r, hd, h * 512:h * 512 + 512], bank(b)[r, :], ACT.Copy,
                                         scale=QSCALE).then_inc(g("q_high"), 1)
            elif what == "k":
                nc.scalar.activation(Kh[:, h * 512:h * 512 + n], bank(b, n), ACT.Copy).then_inc(g("k_high"), 1)
            else:
                nc.scalar.activation(bf.vT[:, h * 512:h * 512 + n], bank(b, n), ACT.Copy).then_inc(g("v_copied"), 1)

        def v_high():
            for j in range(nv):
                act.wait_ge(*g("v_turned", pi * nv + j + 1))
                m = min(4, Kn // P)
                src = bank(6 + j, m * P).rearrange("p (t a d) -> p t a d", a=2, d=HD)
                for hd in range(2):
                    ins = nc.scalar.activation(bf.Vh[:, 4 * j:4 * j + m, 2 * HD * hd:2 * HD * hd + HD],
                                               src[:, :, hd, :], ACT.Copy)
                    ins.then_inc(g("v_high"), 1)

        def exp(n):
            w = width(kind, n)
            act.wait_ge(*g("logits", pi * 16 + n + 1))
            p = bf.Pb[:, n % 2, 0:w]
            nc.scalar.activation(p, p, ACT.Exp, bias=mneg[:, n:n + 1], scale=-1.0,
                                 accum_out=den[:, n:n + 1]).then_inc(g("probs"), 1)

        def pt_high(n):
            s = n // 2
            act.wait_ge(*g("turned", pi * 16 + n + 1))
            if s >= 1 and n % 2 == 0:
                act.wait_ge(*g("pv", pi * 8 + s))
            k = width(kind, n) // P
            nc.scalar.activation(PTh[:, 0:k, n % 2, :], bank(4, k * P).rearrange("p (k q) -> p k q", q=P)
                                 if k <= 4 else ps[:, 2048:2048 + k * P].rearrange("p (k q) -> p k q", q=P),
                                 ACT.Copy).then_inc(g("pt_high"), 1)

        exp(0)
        v_high()
        for n in range(16):
            if n + 1 < 16:
                exp(n + 1)
            pt_high(n)
            if n % 4 == 3:
                c = n // 4
                act.wait_ge(*g("rden_turned", pi * 4 + c + 1))
                nc.scalar.activation(bf.RSb[:, :], bank(6 + c % 2, 256, 256), ACT.Copy).then_inc(g("rden_copied"), 1)

    def pair_dve(dve, kind, L, pi, dst):
        g = pair_names(kind)
        bf = MemBuf if kind == "mem" else DilBuf
        Kn = M if kind == "mem" else S
        nv = (Kn // P + 3) // 4
        if kind == "dil":
            for hd in range(2):
                nc.vector.scalar_tensor_tensor(bf.B[:, hd, :], ndist[:, :], slopes[:, bass.ds(pi * 2 + hd, 1)],
                                               logc[:, :], ALU.mult, ALU.add).then_inc(g("bias"), 1)
        nq = 0
        for j, (what, h, b) in enumerate(groups(kind)):
            n = M if what != "q" and kind == "mem" else 512
            if what == "q":
                for hd in range(2):
                    nq += 1
                    dve.wait_ge(*g("q_high", pi * 4 + nq))
                    r = slice(HD * hd, HD * hd + HD)
                    cs = slice(h * 512, h * 512 + 512)
                    nc.vector.scalar_tensor_tensor(bf.Ql[r, hd, cs], bank(b)[r, :], QSCALE,
                                                   bf.Qh[r, hd, cs].bitcast(F32), ALU.mult,
                                                   ALU.subtract).then_inc(g("q_low"), 1)
            elif what == "k":
                dve.wait_ge(*g("k_high", pi * (Kn // min(Kn, 512)) + h + 1))
                cs = slice(h * 512, h * 512 + n)
                nc.vector.tensor_tensor(Kl[:, cs], bank(b, n), Kh[:, cs].bitcast(F32),
                                        ALU.subtract).then_inc(g("k_low"), 1)

        def v_low():
            for j in range(nv):
                dve.wait_ge(*g("v_high", (pi * nv + j + 1) * 2))
                m = min(4, Kn // P)
                src = bank(6 + j, m * P).rearrange("p (t a d) -> p t a d", a=2, d=HD)
                for hd in range(2):
                    vs = (slice(None), slice(4 * j, 4 * j + m), slice(2 * HD * hd, 2 * HD * hd + HD))
                    ins = nc.vector.tensor_tensor(bf.Vl[vs], src[:, :, hd, :], bf.Vh[vs].bitcast(F32), ALU.subtract)
                ins.then_inc(g("v_low"), 1)

        def logits(n):
            qt, hd = tile_of(n)
            w = width(kind, n)
            dve.wait_ge(*g("scores", pi * 16 + n + 1))
            if n == 0:
                dve.wait_ge(*g("v_turned", (pi + 1) * nv))
            if n >= 2:
                dve.wait_ge(*g("turned", pi * 16 + n - 1))
            if kind == "dil":
                if n == 0:
                    dve.wait_ge(*g("bias", (pi + 1) * 2))
                bias = bf.B[:, hd, S - P - qt * P:S - P - qt * P + w]
            else:
                bias = bf.zero[:, :]
            nc.vector.memset(tick[:, n:n + 1], 0.0)
            o = bf.Pb[:, n % 2, 0:w]
            if w > 512:
                bias = bias.rearrange("p (a c) -> p a c", a=2)
                o = o.rearrange("p (a c) -> p a c", a=2)
            nc.vector.tensor_tensor_reduce(o, s_view(kind, n), bias, -1.0, 3e38, ALU.add, ALU.min,
                                           mneg[:, n:n + 1]).then_inc(g("logits"), 1)

        def pt_low(n):
            dve.wait_ge(*g("pt_high", pi * 16 + n + 1))
            k = width(kind, n) // P
            nc.vector.tensor_tensor(PTl[:, 0:k, n % 2, :], ps[:, 2048:2048 + k * P].rearrange("p (k q) -> p k q", q=P),
                                    PTh[:, 0:k, n % 2, :].bitcast(F32), ALU.subtract).then_inc(g("pt_low"), 1)

        def zero(s):
            if s >= 1:
                dve.wait_ge(*g("pv", pi * 8 + s))
            k = 2 * (s // 2) + 1
            nc.vector.memset(PTh[:, k, 0, :].bitcast(F32), 0.0).then_inc(g("pt_zero"), 1)
            nc.vector.memset(PTl[:, k, 0, :].bitcast(F32), 0.0).then_inc(g("pt_zero"), 1)

        logits(0)
        v_low()
        for n in range(16):
            if n + 1 < 16:
                logits(n + 1)
            if kind == "dil" and n % 2 == 0:
                zero(n // 2)
            pt_low(n)
            if n % 4 == 3:
                c = n // 4
                t0 = 4 * c
                dve.wait_ge(*g("probs", pi * 16 + n + 1))
                if c >= 1:
                    dve.wait_ge(*g("rden_turned", pi * 4 + c))
                nc.vector.reciprocal(rden[:, t0:t0 + 4], den[:, t0:t0 + 4]).then_inc(g("rden"), 1)
                dve.wait_ge(*g("rden", pi * 4 + c + 1))
                src = rden[:, t0:t0 + 4].rearrange("p (h i) -> p i h", h=2).unsqueeze(3).to_broadcast([P, 2, 2, HD])
                nc.vector.tensor_copy(bf.RB[:, :, :, :], src).then_inc(g("rden_wide"), 1)
                dve.wait_ge(*g("rden_copied", pi * 4 + c + 1))
                nc.vector.tensor_tensor(dst(pi, c), bank(6 + c % 2, 256), bf.RSb[:, :],
                                        ALU.mult).then_inc(g("mixed"), 1)

    def mem_dst(pi, c):
        return MO[:, pi % NMP, c * 256:(c + 1) * 256]

    def dil_dst(pi, c):
        return mixT[:, bass.ds(pi, 1), c * 256:(c + 1) * 256].rearrange("p a c -> p (a c)")

    def turn_pe(pe, g, t, src, nk=KT, bb=0):
        if t >= 2:
            pe.wait_ge(*g("xt_low", t - 1))
        b = bb + 2 * (t % 2)
        for k in range(nk):
            mm = nc.tensor.transpose(bank(b + k // 4, P, (k % 4) * P), src[:, k * P:(k + 1) * P], ident[:, :])
        mm.then_inc(g("xt_turned"), 1)

    def turned(t, nk, bb):
        b = bb + 2 * (t % 2)
        return ps[:, 512 * b:512 * b + nk * P].rearrange("p (k q) -> p k q", q=P)

    def turn_act(act, g, t, nk=KT, bb=0, high=XTh):
        act.wait_ge(*g("xt_turned", t + 1))
        nc.scalar.activation(high[:, 0:nk, t * P:(t + 1) * P], turned(t, nk, bb), ACT.Copy).then_inc(g("xt_high"), 1)

    def turn_dve(dve, g, t, nk=KT, bb=0, high=XTh, low=XTl):
        dve.wait_ge(*g("xt_high", t + 1))
        nc.vector.tensor_tensor(low[:, 0:nk, t * P:(t + 1) * P], turned(t, nk, bb),
                                high[:, 0:nk, t * P:(t + 1) * P].bitcast(F32), ALU.subtract).then_inc(g("xt_low"), 1)

    def acc_pe(pe, g, c, u, lhs, slots, ready, after=None):
        pe.wait_ge(split_done, u + 2)
        for t in range(NT):
            ready(t)
            for h in range(2):
                n = 2 * t + h
                if not (isinstance(c, int) and c * 16 + n < 4):
                    pe.wait_ge(*g("added", c * 16 + n - 3 + g.credit))
                for k in range(2):
                    lh, ll = lhs(k, t)
                    mm = three(bank(4 + n % 4), lh, ll, Wh[:, slots[k], h * 512:(h + 1) * 512],
                               Wl[:, slots[k], h * 512:(h + 1) * 512], k == 0, k == 1)
                mm.then_inc(g("product"), 1)
            if after:
                after(t)

    def acc_dve(dve, g, c, t, scaled=None):
        for h in range(2):
            n = 2 * t + h
            dve.wait_ge(*g("product", c * 16 + n + 1))
            x = XR[:, t, h * 512:(h + 1) * 512]
            if scaled:
                nc.vector.scalar_tensor_tensor(x, x, scaled, bank(4 + n % 4), ALU.mult, ALU.add).then_inc(g("added"), 1)
            else:
                nc.vector.tensor_tensor(x, x, bank(4 + n % 4), ALU.add).then_inc(g("added"), 1)

    SKEW = 3

    def norm_pe_after(pe, g):
        def after(t):
            if t >= SKEW:
                pe.wait_ge(*g("shifted", t - SKEW + 1))
                turn_pe(pe, g, t - SKEW, XR[:, t - SKEW, :])
        return after

    def norm_pe_rest(pe, g):
        for t in range(NT - SKEW, NT):
            pe.wait_ge(*g("shifted", t + 1))
            turn_pe(pe, g, t, XR[:, t, :])

    def norm_dve(dve, g, c, last, scaled=None):
        nself = 0
        for t in range(NT + SKEW):
            if t < NT:
                acc_dve(dve, g, c, t, scaled)
                dve.wait_ge(*g("added", c * 16 + 2 * t + 2 + g.credit))
                for h in range(2):
                    nc.vector.bn_stats(st[:, t, h, :], XR[:, t, h * 512:(h + 1) * 512]).then_inc(g("ln_self"), 1)
                nself += 2
                dve.wait_ge(*g("ln_self", nself))
                nc.vector.bn_aggr(mv[:, t, :], st[:, t, 0:2, :].rearrange("p a b -> p (a b)")).then_inc(g("stats"), 1)
            if 1 <= t <= NT:
                q = t - 1
                dve.wait_ge(*g("root", t))
                nc.vector.reciprocal(rstd[:, q:q + 1], rstd[:, q:q + 1]).then_inc(g("ln_self"), 1)
                nself += 1
                dve.wait_ge(*g("ln_self", nself))
                nc.vector.tensor_scalar(nmr[:, q:q + 1], mv[:, q, 0:1], rstd[:, q:q + 1], -1.0, ALU.mult,
                                        ALU.mult).then_inc(g("rstd"), 1)
            if t >= SKEW and not last:
                turn_dve(dve, g, t - SKEW)

    def norm_act(act, g, last):
        for t in range(NT + SKEW):
            if t < NT:
                act.wait_ge(*g("stats", t + 1))
                nc.scalar.activation(rstd[:, t:t + 1], mv[:, t, 1:2], ACT.Sqrt, bias=eps[:, 0:1]).then_inc(g("root"), 1)
            if 1 <= t <= NT:
                q = t - 1
                act.wait_ge(*g("rstd", t))
                nc.scalar.activation(XR[:, q, :], XR[:, q, :], ACT.Identity, bias=nmr[:, q:q + 1],
                                     scale=rstd[:, q:q + 1]).then_inc(g("normed"), 1)
            if t >= SKEW and not last:
                q = t - SKEW
                turn_act(act, g, q)
                nc.scalar.activation(XR[:, q, :], XR[:, q, :], ACT.Copy, scale=ALPHA).then_inc(g("scaled"), 1)

    def norm_pool(pool, g):
        pool.wait_ge(*g("gb_landed", 32))
        for t in range(NT):
            pool.wait_ge(*g("normed", t + 1))
            nc.gpsimd.tensor_tensor(XR[:, t, :], XR[:, t, :], gb[:, 0, :], ALU.mult).then_inc(g("gained"), 1)
            pool.wait_ge(*g("gained", t + 1))
            nc.gpsimd.tensor_tensor(XR[:, t, :], XR[:, t, :], gb[:, 1, :], ALU.add).then_inc(g("shifted"), 1)

    def load_gb(eng, g, gain, shift, dst):
        n = dst.shape[2]
        for i, w in enumerate((gain, shift)):
            eng.dma_start(dst[:, i, :], w.rearrange("(a n) -> a n", a=1).to_broadcast([P, n])).then_inc(g("gb_landed"), 16)

    class Names:
        def __init__(self, phase, rises=(), layer=0, credit=0):
            self.phase, self.rises, self.layer, self.credit = phase, dict(rises), layer, credit

        def __call__(self, name, value=None):
            s = sem(f"{self.phase}_{name}")
            return s if value is None else (s, value + self.layer * self.rises.get(name, 0))

    NORM = {"xt_turned": NT, "xt_high": NT, "xt_low": NT, "stats": NT, "root": NT, "rstd": NT, "normed": NT,
            "scaled": NT, "gained": NT, "shifted": NT, "ln_self": 3 * NT, "gb_landed": 32}
    OUT = {**NORM, "product": 16 * KT // 2, "added": 16 * KT // 2}
    FFN = {**NORM, "product": 16 * NCH, "added": 16 * NCH,
           **{x: 4 * NCH for x in ("gate", "up", "silu", "gated", "hid_high", "hid_low")}}
    gi = Names("in")
    gm = [Names("memory", {"xt_turned": 2, "xt_high": 2, "xt_low": 2}, L) for L in range(2)]
    go = [Names("out", OUT, L) for L in range(2)]
    gf = [Names("ffn", FFN, L, 4) for L in range(2)]

    def ffn_slots(L):
        return [(U_FFN[L] + j) % WS for j in range(6)]

    def ffn_pe(pe, L, c, last):
        g = gf[L]
        sl = ffn_slots(L)
        u = U_FFN[L] + c * 6
        for h in range(2):
            for m in range(2):
                i = 2 * h + m
                if h == 0:
                    pe.wait_ge(split_done, u + 2 * m + 2)
                pe.wait_ge(*g("gated", c * 4 + i - 2 + 1 + 2))
                rows_in(bank(2 * (i % 2)), sl[2 * m], XTh, XTl, h * 512, 512).then_inc(g("gate"), 1)
                rows_in(bank(2 * (i % 2) + 1), sl[2 * m + 1], XTh, XTl, h * 512, 512).then_inc(g("up"), 1)

        def ready(t):
            if t % 4 == 0:
                pe.wait_ge(*g("hid_low", c * 4 + 2 * (t // 4) + 2 + 2))

        acc_pe(pe, g, c, u + 4, lambda k, t: (hidh[:, k, t * P:(t + 1) * P], hidl[:, k, t * P:(t + 1) * P]),
               sl[4:6], ready, after=norm_pe_after(pe, g) if last and L == 0 else None)

    def ffn_act(act, L, c):
        g = gf[L]
        for i in range(4):
            h, m = i // 2, i % 2
            act.wait_ge(*g("gate", c * 4 + i + 1))
            act.wait_ge(*g("gated", c * 4 + i - 2 + 1 + 2))
            nc.scalar.activation(silu[:, i % 2, :], bank(2 * (i % 2)), ACT.Silu).then_inc(g("silu"), 1)
            act.wait_ge(*g("gated", c * 4 + i + 1 + 2))
            nc.scalar.activation(hidh[:, m, h * 512:(h + 1) * 512], hid[:, i % 2, :], ACT.Copy).then_inc(g("hid_high"), 1)

    def ffn_dve(dve, L, c, last):
        g = gf[L]
        for i in range(4):
            h, m = i // 2, i % 2
            dve.wait_ge(*g("silu", c * 4 + i + 1))
            dve.wait_ge(*g("up", c * 4 + i + 1))
            dve.wait_ge(*g("hid_low", c * 4 + i - 2 + 1 + 2))
            nc.vector.tensor_tensor(hid[:, i % 2, :], silu[:, i % 2, :], bank(2 * (i % 2) + 1),
                                    ALU.mult).then_inc(g("gated"), 1)
            dve.wait_ge(*g("hid_high", c * 4 + i + 1))
            nc.vector.tensor_tensor(hidl[:, m, h * 512:(h + 1) * 512], hid[:, i % 2, :],
                                    hidh[:, m, h * 512:(h + 1) * 512].bitcast(F32),
                                    ALU.subtract).then_inc(g("hid_low"), 1)
        if not last:
            for t in range(NT):
                acc_dve(dve, g, c, t)

    gvp, gup, gsg = Names("vproj"), Names("uproj"), Names("sgu")

    def wide_pe(pe, g, u, free, after):
        for t in range(NT):
            for j in range(3):
                n = 3 * t + j
                if t == 0:
                    pe.wait_ge(split_done, u + 2 * j + 2)
                if n >= 4:
                    pe.wait_ge(*g("gelu", n - 3))
                s0 = (u + 2 * j) % WS
                dst = bank(n % 4, M).rearrange("p (a c) -> p a c", c=P)
                for k in range(KT):
                    mm = three(dst, XTh[:, k, t * P:(t + 1) * P], XTl[:, k, t * P:(t + 1) * P],
                               Wh[:, s0:s0 + 2, k * P:(k + 1) * P], Wl[:, s0:s0 + 2, k * P:(k + 1) * P],
                               k == 0, k == KT - 1)
                mm.then_inc(g("product"), 1)
            after(t)

    def turn_ws(pe):
        pe.wait_ge(*gsg("lower", 1))
        for i in range(NG):
            mm = nc.tensor.transpose(bank(4 + i // 4, P, (i % 4) * P), wsraw[:, i, :], ident[:, :])
        mm.then_inc(gsg("ws_turned"), 1)

    def sgu_pe(pe):
        wide_pe(pe, gvp, U_V, None, lambda t: turn_ws(pe) if t == 3 else None)
        pe.wait_ge(*gsg("ws_low", 1))
        for i in range(NG):
            pe.wait_ge(*gsg("v_low", i + 1))
            if i >= 4:
                pe.wait_ge(*gsg("gate", i - 3))
            three(bank(4 + i % 4), WSh[:, i, :], WSl[:, i, :],
                  VSh[:, i % 2, :, :].rearrange("p a b -> p (a b)"),
                  VSl[:, i % 2, :, :].rearrange("p a b -> p (a b)"), True, True).then_inc(gsg("spatial"), 1)
        pe.wait_ge(*gsg("gate", NG))

        def after(t):
            if t >= 1:
                pe.wait_ge(*gup("gated", 3 * t))
                turn_pe(pe, gup, t - 1, V[:, t - 1, :], DIL_W // P, 4)

        wide_pe(pe, gup, U_U, None, after)
        pe.wait_ge(*gup("gated", 3 * NT))
        turn_pe(pe, gup, NT - 1, V[:, NT - 1, :], DIL_W // P, 4)

    def sgu_act(act):
        act.wait_ge(sem("mem_mixed"), 8 * NMP + 1)
        act.dma_start(wsraw[:, :, :], a["sgu_w_s"][0].rearrange("g t s -> t g s")).then_inc(gsg("ws_landed"), 16)
        with nc.allow_non_contiguous_dma(reason="1536 biases, once"):
            act.dma_start(bst[:, :], a["sgu_b_s"][0].rearrange("g t -> t g")).then_inc(gsg("bs_landed"), 16)

        for n in range(3 * NT):
            act.wait_ge(*gvp("product", n + 1))
            nc.scalar.activation(V[:, n // 3, (n % 3) * M:(n % 3 + 1) * M], bank(n % 4, M),
                                 ACT.Gelu_apprx_tanh).then_inc(gvp("gelu"), 1)
            if n == 17:
                act.wait_ge(*gsg("ws_turned", 1))
                nc.scalar.activation(WSh[:, :, :], ps[:, 2048:2048 + NG * P].rearrange("p (g t) -> p g t", t=P),
                                     ACT.Copy).then_inc(gsg("ws_high"), 1)
                load_gb(act, gsg, a["sgu_ln_g"][0], a["sgu_ln_b"][0], sgb)
        act.wait_ge(*gsg("stats", NT))
        nc.scalar.activation(rstd[:, :], mv[:, :, 1], ACT.Sqrt, bias=eps[:, 0:1]).then_inc(gsg("root"), 1)
        act.wait_ge(*gsg("shifted", NT))
        for i in range(NG):
            if i >= 2:
                act.wait_ge(*gsg("spatial", i - 1))
            nc.scalar.activation(VSh[:, i % 2, :, :], V[:, :, i * HD:(i + 1) * HD], ACT.Copy).then_inc(gsg("v_high"), 1)
        act.wait_ge(*gsg("spatial", NG))
        load_gb(act, go[1], a["ln_mix_g"][1], a["ln_mix_b"][1], gb)
        for n in range(3 * NT + 3):
            if n < 3 * NT:
                act.wait_ge(*gup("product", n + 1))
                if n >= 2:
                    act.wait_ge(*gup("gated", n - 1))
                nc.scalar.activation(ub[:, n % 2, :], bank(n % 4, M), ACT.Gelu_apprx_tanh).then_inc(gup("gelu"), 1)
            if n % 3 == 2 and n >= 5:
                t = n // 3 - 1
                ts = slice(t * P, (t + 1) * P)
                turn_act(act, gup, t, DIL_W // P, 4)
                nc.scalar.activation(XTh[:, 6:8, ts], MO[:, :, ts], ACT.Copy).then_inc(gup("mo_high"), 1)

    def sgu_dve(dve):
        for t in range(NT):
            for j in range(3):
                dve.wait_ge(*gvp("gelu", 3 * t + j + 1))
                nc.vector.bn_stats(st[:, t, j, :], V[:, t, j * M:(j + 1) * M]).then_inc(gsg("partial"), 1)
            dve.wait_ge(*gsg("partial", 3 * t + 3))
            nc.vector.bn_aggr(mv[:, t, :], st[:, t, :, :].rearrange("p a b -> p (a b)")).then_inc(gsg("stats"), 1)
            if t == 5:
                dve.wait_ge(*gsg("ws_high", 1))
                nc.vector.tensor_tensor(WSl[:, :, :], ps[:, 2048:2048 + NG * P].rearrange("p (g t) -> p g t", t=P),
                                        WSh[:, :, :].bitcast(F32), ALU.subtract).then_inc(gsg("ws_low"), 1)
        dve.wait_ge(*gsg("root", 1))
        nc.vector.reciprocal(rstd[:, :], rstd[:, :]).then_inc(gsg("rstd"), 1)
        dve.wait_ge(*gsg("rstd", 1))
        dve.wait_ge(*gsg("gb_landed", 32))
        for t in range(NT):
            nc.vector.tensor_scalar(V[:, t, :], V[:, t, :], mv[:, t, 0:1], rstd[:, t:t + 1], ALU.subtract,
                                    ALU.mult).then_inc(gsg("normed"), 1)
            dve.wait_ge(*gsg("normed", t + 1))
            nc.vector.tensor_tensor(V[:, t, :], V[:, t, :], sgb[:, 0, :], ALU.mult).then_inc(gsg("gained"), 1)
        dve.wait_ge(*gsg("bs_landed", 16))
        for i in range(NG + 1):
            if i < NG:
                dve.wait_ge(*gsg("v_high", i + 1))
                nc.vector.tensor_tensor(VSl[:, i % 2, :, :], V[:, :, i * HD:(i + 1) * HD],
                                        VSh[:, i % 2, :, :].bitcast(F32), ALU.subtract).then_inc(gsg("v_low"), 1)
            if i >= 1:
                q = i - 1
                dve.wait_ge(*gsg("spatial", q + 1))
                nc.vector.tensor_scalar(V[:, :, q * HD:(q + 1) * HD],
                                        bank(4 + q % 4).rearrange("p (t c) -> p t c", c=HD), bst[:, q:q + 1], None,
                                        ALU.add).then_inc(gsg("gate"), 1)
        dve.wait_ge(*gsg("gate", NG))
        for n in range(3 * NT + 3):
            if n < 3 * NT:
                dve.wait_ge(*gup("gelu", n + 1))
                v = V[:, n // 3, (n % 3) * M:(n % 3 + 1) * M]
                nc.vector.tensor_tensor(v, v, ub[:, n % 2, :], ALU.mult).then_inc(gup("gated"), 1)
            if n % 3 == 2 and n >= 5:
                t = n // 3 - 1
                ts = slice(t * P, (t + 1) * P)
                turn_dve(dve, gup, t, DIL_W // P, 4)
                dve.wait_ge(*gup("mo_high", t + 1))
                nc.vector.tensor_tensor(XTl[:, 6:8, ts], MO[:, :, ts], XTh[:, 6:8, ts].bitcast(F32),
                                        ALU.subtract).then_inc(gup("mo_low"), 1)

    def sgu_pool(pool):
        pool.wait_ge(*gsg("ws_landed", 16))
        nc.gpsimd.affine_select(out=wsraw[:, :, :], in_=wsraw[:, :, :], compare_op=ALU.is_ge, fill=0.0, base=0,
                                pattern=[[0, NG], [-1, P]], channel_multiplier=1).then_inc(gsg("lower"), 1)
        for t in range(NT):
            pool.wait_ge(*gsg("gained", t + 1))
            nc.gpsimd.tensor_tensor(V[:, t, :], V[:, t, :], sgb[:, 1, :], ALU.add).then_inc(gsg("shifted"), 1)

    MEMSL = DILSL = [0, 1, 2]
    block = nc.Block()
    block.__enter__()

    @block.sync
    def _(sp):
        w = [a["a_w_in"][0], a["b_w_in"][0]]
        mem_q = [3 * DIL_W, 2 * DIL_W]

        def mem_units(L):
            for p in range(NMP):
                u = U_MEM[L] + 3 * p
                load(sp, u, cols(w[L], mem_q[L] + p * P))
                load(sp, u + 1, cols(a["w_mem_kv"][L], p * P))
                load(sp, u + 2, cols(a["w_mem_kv"][L], MEM_W + p * P))

        def out_units(L):
            for k in range(KT):
                load(sp, U_OUT[L] + k, a["w_out"][L][k * P:(k + 1) * P, :])

        def ffn_units(L):
            with sp.Fori(0, NCH) as c:
                u = U_FFN[L] + c * 6
                for m in range(2):
                    load(sp, u + 2 * m, cols(a["w_gate"][L], c * 256 + m * P))
                    load(sp, u + 2 * m + 1, cols(a["w_up"][L], c * 256 + m * P))
                for k in range(2):
                    load(sp, u + 4 + k, a["w_down"][L][bass.ds(c * 256 + k * P, P), :])

        mem_units(0)
        for p in range(NDP):
            for j in range(3):
                load(sp, U_DIL + 3 * p + j, cols(w[0], j * DIL_W + p * P))
        out_units(0)
        ffn_units(0)
        mem_units(1)
        for j in range(6):
            load(sp, U_V + j, cols(w[1], DIL_W + j * P))
        for j in range(6):
            load(sp, U_U + j, cols(w[1], j * P))
        out_units(1)
        ffn_units(1)
        for t in range(NT):
            sp.wait_ge(*gf[1]("shifted", t + 1))
            sp.dma_start(out[0, t * P:(t + 1) * P, :], XR[:, t, :]).then_inc(sem("stored"), 16)
        sp.wait_ge(sem("stored"), 16 * NT)

    @block.gpsimd
    def _(pool):
        nc.gpsimd.memset(zcol[:, :], 0.0).then_inc(sem("zcol_set"), 1)
        pool.wait_ge(sem("zcol_set"), 1)
        for j in range(6):
            split(pool, j, j % 3, j - 3 if j >= 3 else None)
        for j in range(3 * NDP):
            split(pool, U_DIL + j, j % 3, U_DIL + j - 3)
        for k in range(KT):
            u = U_OUT[0] + k
            slot = u % WS
            if k < 3:
                before = u - 3
            elif k < 6:
                before = (sem("dil_mixed"), 4 * NDP + 1)
            else:
                before = u - 6
            split(pool, u, slot, before)

        def ffn_units(L):
            for j in range(4):
                split(pool, U_FFN[L] + j, (U_FFN[L] + j) % WS, U_FFN[L] + j - 6)
            norm_pool(pool, go[L])
            for j in range(4, 6):
                split(pool, U_FFN[L] + j, (U_FFN[L] + j) % WS, U_FFN[L] + j - 6)
            with pool.Fori(1, NCH) as c:
                for j in range(6):
                    split(pool, U_FFN[L] + c * 6 + j, (U_FFN[L] + j) % WS, used(U_FFN[L] + j, c - 1),
                          (U_FFN[L] + j) % RS, U_FFN[L] // 2 + c * 3 + j // 2 + 1)

        ffn_units(0)
        for j in range(6):
            if j == 1:
                norm_pool(pool, gf[0])
            u = U_MEM[1] + j
            split(pool, u, u % 3, {98: 92, 99: 96, 100: 97}.get(u, u - 3))
        for j in range(6):
            u = U_V + j
            before = {104: 101, 108: 102, 109: 103}.get(u)
            split(pool, u, u % WS, before if before else (sem("mem_mixed"), 8 * NMP + 1))
        sgu_pool(pool)
        for j in range(6):
            split(pool, U_U + j, (U_U + j) % WS, U_U + j - 6)
        for k in range(KT):
            split(pool, U_OUT[1] + k, (U_OUT[1] + k) % WS, U_OUT[1] + k - 6)
        ffn_units(1)
        norm_pool(pool, gf[1])

    @block.tensor
    def _(pe):
        pe.wait_ge(sem("const_landed"), 32)
        for t in range(NT):
            if t % 2 == 0:
                pe.wait_ge(sem(f"x_landed{t // 2}"), 16)
            turn_pe(pe, gi, t, XR[:, t, :])
        before = gi
        for L in range(2):
            pe.wait_ge(*before("xt_low", NT))
            pe.wait_ge(sem(f"mem_landed{L}"), 16)
            for t in range(2):
                turn_pe(pe, gm[L], t, memraw[:, t, :])
            pe.wait_ge(*gm[L]("xt_low", 2))
            for p in range(NMP):
                pair_pe(pe, "mem", L, NMP * L + p, U_MEM[L] + 3 * p, [(U_MEM[L] + j) % 3 for j in range(3)])
            if L == 0:
                pe.wait_ge(sem("mem_mixed"), 4 * NMP + 1)
                with pe.Fori(0, NDP) as p:
                    pair_pe(pe, "dil", 0, p, p * 3 + U_DIL, DILSL)
                pe.wait_ge(sem("dil_mixed"), 4 * NDP + 1)
            else:
                pe.wait_ge(sem("mem_mixed"), 8 * NMP + 1)
                sgu_pe(pe)
                pe.wait_ge(*gup("xt_low", NT))

            for c in range(KT // 2):
                def ready(t):
                    if L == 0 and t == 0:
                        pe.wait_ge(sem("mix_low"), 2 * c + 2)
                    if L == 1 and c == 0:
                        pe.wait_ge(*gup("mo_low", t + 1))
                u = U_OUT[L] + 2 * c
                acc_pe(pe, go[L], c, u,
                       lambda k, t: (XTh[:, 2 * c + k, t * P:(t + 1) * P], XTl[:, 2 * c + k, t * P:(t + 1) * P]),
                       [u % WS, (u + 1) % WS], ready, after=norm_pe_after(pe, go[L]) if c == 3 else None)
            norm_pe_rest(pe, go[L])
            pe.wait_ge(*go[L]("xt_low", NT))
            with pe.Fori(0, NCH - 1) as c:
                ffn_pe(pe, L, c, False)
            ffn_pe(pe, L, NCH - 1, True)
            if L == 0:
                norm_pe_rest(pe, gf[L])
            before = gf[L]

    @block.scalar
    def _(act):
        for i in range(4):
            act.dma_start(XR[:, 2 * i:2 * i + 2, :], a["x"][0, 256 * i:256 * i + 256, :].rearrange("(t p) d -> p t d", p=P)
                          ).then_inc(sem(f"x_landed{i}"), 16)
            if i == 0:
                act.dma_start(ident[:, :], a["c_ident"]).then_inc(sem("const_landed"), 16)
                act.dma_start(slopes[:, :], a["c_slopes"]).then_inc(sem("const_landed"), 16)
        mem = a["mem"][0].rearrange("(t p) d -> p t d", p=P)
        act.dma_start(memraw[:, :, :], mem).then_inc(sem("mem_landed0"), 16)
        for t in range(NT):
            turn_act(act, gi, t)
        for L in range(2):
            for t in range(2):
                turn_act(act, gm[L], t, high=memTh)
            for p in range(NMP):
                pair_act(act, "mem", L, NMP * L + p)
            if L == 0:
                act.wait_ge(sem("mem_mixed"), 4 * NMP + 1)
                act.dma_start(ndist[:, :], a["c_ndist"]).then_inc(sem("table_landed"), 16)
                act.dma_start(logc[:, :], a["c_logc"]).then_inc(sem("table_landed"), 16)
                with act.Fori(0, NDP) as p:
                    pair_act(act, "dil", 0, p)
                act.wait_ge(sem("dil_mixed"), 4 * NDP + 1)
                for i in range(4):
                    act.dma_start(XR[:, 2 * i:2 * i + 2, :],
                                  a["x"][0, 256 * i:256 * i + 256, :].rearrange("(t p) d -> p t d", p=P)
                                  ).then_inc(sem(f"x_again{i}"), 16)
                load_gb(act, go[0], a["ln_mix_g"][0], a["ln_mix_b"][0], gb)
                for j in range(KT):
                    src = mixT[:, j, :] if j < NDP else MO[:, j - NDP, :]
                    nc.scalar.activation(XTh[:, j, :], src, ACT.Copy).then_inc(sem("mix_high"), 1)
            else:
                sgu_act(act)
            norm_act(act, go[L], False)
            act.wait_ge(*go[L]("shifted", NT))
            load_gb(act, gf[L], a["ln_ffn_g"][L], a["ln_ffn_b"][L], gb)
            if L == 0:
                act.wait_ge(sem("mix_low"), KT)
                act.dma_start(memraw[:, :, :], mem).then_inc(sem("mem_landed1"), 16)
            with act.Fori(0, NCH) as c:
                ffn_act(act, L, c)
            norm_act(act, gf[L], L == 1)

    @block.vector
    def _(dve):
        def attention_start(g, bf, times=1):
            for q in (bf.Qh, bf.Ql):
                nc.vector.memset(q[HD:P, 0, :].bitcast(F32), 0.0).then_inc(g("cleared"), 1)
                nc.vector.memset(q[0:HD, 1, :].bitcast(F32), 0.0).then_inc(g("cleared"), 1)
            for v in (bf.Vh, bf.Vl):
                nc.vector.memset(v[:, :, HD:2 * HD].bitcast(F32), 0.0).then_inc(g("cleared"), 1)
            dve.wait_ge(*g("cleared", 6 * times))
            if times == 1:
                dve.sem_inc(g("mixed"), 1)

        nc.vector.memset(eps[:, :], EPS).then_inc(sem("eps_set"), 1)
        for t in range(NT):
            turn_dve(dve, gi, t)
        for L in range(2):
            for t in range(2):
                turn_dve(dve, gm[L], t, high=memTh, low=memTl)
            g = pair_names("mem")
            dve.wait_ge(*gm[L]("xt_low", 2))
            nc.vector.memset(MemBuf.zero[:, :], 0.0).then_inc(g("zeroed"), 1)
            dve.wait_ge(*g("zeroed", L + 1))
            attention_start(g, MemBuf, L + 1)
            for p in range(NMP):
                pair_dve(dve, "mem", L, NMP * L + p, mem_dst)
            if L == 0:
                g = pair_names("dil")
                dve.wait_ge(sem("mem_mixed"), 4 * NMP + 1)
                attention_start(g, DilBuf)
                dve.wait_ge(sem("table_landed"), 32)
                with dve.Fori(0, NDP) as p:
                    pair_dve(dve, "dil", 0, p, dil_dst)
                for j in range(KT):
                    src = mixT[:, j, :] if j < NDP else MO[:, j - NDP, :]
                    dve.wait_ge(sem("mix_high"), j + 1)
                    nc.vector.tensor_tensor(XTl[:, j, :], src, XTh[:, j, :].bitcast(F32),
                                            ALU.subtract).then_inc(sem("mix_low"), 1)
            else:
                sgu_dve(dve)
            for c in range(KT // 2 - 1):
                for t in range(NT):
                    if L == 0 and c == 0 and t % 2 == 0:
                        dve.wait_ge(sem(f"x_again{t // 2}"), 16)
                    acc_dve(dve, go[L], c, t, ALPHA if L == 0 and c == 0 else None)
            norm_dve(dve, go[L], KT // 2 - 1, False)
            if L == 0:
                dve.sem_inc(gf[L]("gated"), 2)
            if L == 0:
                dve.sem_inc(gf[L]("hid_low"), 2)
            if L == 0:
                dve.sem_inc(gf[L]("added"), 4)
            with dve.Fori(0, NCH - 1) as c:
                ffn_dve(dve, L, c, False)
            ffn_dve(dve, L, NCH - 1, True)
            norm_dve(dve, gf[L], NCH - 1, L == 1)

    block.__exit__(None, None, None)


_INS = ["x", "mem", "a_w_in", "b_w_in", "sgu_ln_g", "sgu_ln_b", "sgu_w_s", "sgu_b_s", "w_mem_kv", "w_out",
        "ln_mix_g", "ln_mix_b", "w_gate", "w_up", "w_down", "ln_ffn_g", "ln_ffn_b"]


def kernel(**inputs):
    import concourse.bacc as bacc
    from concourse.bass_utils import run_bass_kernel_spmd

    nc = bacc.Bacc("TRN2", target_bir_lowering=False, num_devices=1)
    arrays = {n: np.ascontiguousarray(inputs[n]) for n in _INS}
    arrays.update(zip(("c_ndist", "c_logc", "c_slopes", "c_ident"), tables()))
    a = {n: nc.dram_tensor(f"in_{n}", v.shape, mybir.dt.from_np(v.dtype), kind="ExternalInput").ap()
         for n, v in arrays.items()}
    out = nc.dram_tensor("out_0", (1, S, D), F32, kind="ExternalOutput").ap()
    build(nc, a, out)
    r = run_bass_kernel_spmd(nc, [{f"in_{n}": v for n, v in arrays.items()}], core_ids=[0])
    return r.results[0]["out_0"]
```

```python
import numpy as np
import concourse.bass as bass
import concourse.mybir as mybir

F32 = mybir.dt.float32
F32R = mybir.dt.float32r
ALU = mybir.AluOpType
ACT = mybir.ActivationFunctionType

P = 128
S = 1024
D = 1024
M = 256
HD = 64
NT = S // P
KT = D // P
DIL_W = 768
MEM_W = 256
NDP = DIL_W // P
NMP = MEM_W // P
FF = 2816
NG = DIL_W // HD
NCH = FF // (2 * P)
ALPHA = float((2 * 2) ** 0.25)
EPS = 1e-5
PATTERNS = ((128, 1), (512, 4), (2048, 16))
UNIT = 1024
WS = 6
RS = 2
QSCALE = HD ** -0.5

U_MEM = (0, 98)
U_DIL = 6
U_V, U_U = 104, 110
U_OUT = (24, 116)
U_FFN = (32, 124)
U_END = 190

KB = 1024
A_XTH, A_XTL, A_XR = 0, 32 * KB, 64 * KB
A_WH, A_WL, A_RAW = 96 * KB, 120 * KB, 144 * KB
A_MV, A_MO, A_X = 152 * KB, 176 * KB, 184 * KB
A_SMALL = 206 * KB


def tables():
    d = (np.arange(P)[:, None] - np.arange(S)[None, :] + (S - P)).astype(np.int64)
    count = np.zeros(d.shape, np.int64)
    for window, dil in PATTERNS:
        count += (d >= 0) & (d <= window) & (d % dil == 0)
    slopes = np.exp2(-8.0 * (np.arange(NG) + 1.0) / NG).astype(np.float32)
    bias = np.where(count > 0, np.log(np.maximum(count, 1)) - slopes[:, None, None].astype(np.float64) * d, -1e30)
    return bias.astype(np.float32), np.eye(P, dtype=np.float32)


def build(nc, a, out):
    base = -(-nc.sbuf_base // 64) * 64

    def at(name, shape, dt, off):
        return nc.alloc_sbuf_tensor_at(name, shape, dt, offset=base + off)

    sems = {}

    def sem(name):
        if name not in sems:
            sems[name] = nc.alloc_semaphore(name)
        return sems[name]

    XTh = at("XTh", [P, KT, S], F32R, A_XTH)
    XTl = at("XTl", [P, KT, S], F32R, A_XTL)
    XR = at("XR", [P, NT, D], F32, A_XR)
    Wh = at("Wh", [P, WS, UNIT], F32R, A_WH)
    Wl = at("Wl", [P, WS, UNIT], F32R, A_WL)
    raw = at("raw", [P, RS, UNIT], F32, A_RAW)
    PTh = at("PTh", [P, 2, 4, 2, P], F32R, A_WH + 12 * KB)
    Kh = at("Kh", [P, S], F32R, A_WH + 20 * KB)
    PTl = at("PTl", [P, 2, 4, 2, P], F32R, A_WL + 12 * KB)
    Kl = at("Kl", [P, S], F32R, A_WL + 20 * KB)
    mixT = at("mixT", [P, NDP, S], F32, A_MV)
    MO = at("MO", [P, NMP, S], F32, A_MO)
    memTh = at("memTh", [P, KT, M], F32R, A_MV)
    memTl = at("memTl", [P, KT, M], F32R, A_MV + 8 * KB)
    memraw = at("memraw", [P, 2, D], F32, A_MV + 16 * KB)

    class MemBuf:
        Qh = at("mQh", [P, 2, S], F32R, A_X)
        Ql = at("mQl", [P, 2, S], F32R, A_X + 8 * KB)
        Vh = at("mVh", [P, 2, 192], F32R, A_MV + 16 * KB)
        Vl = at("mVl", [P, 2, 192], F32R, A_MV + 16 * KB + 1536)
        Pb = at("mP", [P, 3, M], F32, A_MV + 19 * KB)
        vT = at("mvT", [P, M], F32, A_MV + 22 * KB)
        RB = at("mRB", [P, 2, 2, HD], F32, A_X + 16 * KB)
        RSb = at("mRS", [P, 2 * P], F32, A_X + 17 * KB)
        zero = at("mzero", [P, M], F32, A_X + 18 * KB)

    class DilBuf:
        Qh = at("dQh", [P, 2, S], F32R, A_XR)
        Ql = at("dQl", [P, 2, S], F32R, A_XR + 8 * KB)
        Vh = at("dVh", [P, NT, 192], F32R, A_XR + 16 * KB)
        Vl = at("dVl", [P, NT, 192], F32R, A_XR + 22 * KB)
        RB = at("dRB", [P, 2, 2, HD], F32, A_XR + 28 * KB)
        RSb = at("dRS", [P, 2 * P], F32, A_XR + 29 * KB)
        Pb = at("dP", [P, 3, S], F32, A_X)
        B = at("dB", [P, 2, S], F32, A_X + 12 * KB)
        vT = at("dvT", [P, S], F32, A_X + 8 * KB)

    gb = at("gb", [P, 2, D], F32, A_X)
    hidh = at("hidh", [P, 2, S], F32R, A_MV)
    hidl = at("hidl", [P, 2, S], F32R, A_MV + 8 * KB)
    silu = at("silu", [P, 2, 512], F32, A_MO)
    hid = at("hid", [P, 2, 512], F32, A_MO + 4 * KB)
    V = at("V", [P, NT, DIL_W], F32, A_MV)
    WSh = at("WSh", [P, NG, P], F32R, A_X)
    WSl = at("WSl", [P, NG, P], F32R, A_X + 6 * KB)
    wsraw = at("wsraw", [P, NG, P], F32, A_X + 12 * KB)
    sgb = at("sgb", [P, 2, DIL_W], F32, A_X + 12 * KB)
    VSh = at("VSh", [P, 2, NT, HD], F32R, A_X + 12 * KB)
    VSl = at("VSl", [P, 2, NT, HD], F32R, A_X + 16 * KB)
    ub = at("ub", [P, 2, M], F32, A_X + 20 * KB)
    small_at = [A_SMALL]

    def small(name, shape):
        n = 4 * int(np.prod(shape[1:]))
        t = at(name, shape, F32, small_at[0])
        small_at[0] += -(-n // 32) * 32
        return t

    ident = small("ident", [P, P])
    mneg = small("mneg", [P, 16])
    den = small("den", [P, 16])
    rden = small("rden", [P, 16])
    st = small("st", [P, NT, 3, 6])
    mv = small("mv", [P, NT, 2])
    rstd = small("rstd", [P, NT])
    nmr = small("nmr", [P, NT])
    bst = small("bst", [P, NG])
    eps = small("eps", [P, 1])
    zcol = small("zcol", [P, 1])
    tick = small("tick", [P, 16])
    ps = nc.alloc_psum_tensor("ps", [P, 8 * 512], F32)

    def bank(b, n=512, off=0):
        return ps[:, 512 * b + off:512 * b + off + n]

    def cols(w, c0):
        return w[:, bass.ds(c0, P)].rearrange("(k p) c -> p k c", p=P)

    def load(sp, u, src):
        if not (isinstance(u, int) and u < RS):
            sp.wait_ge(split_done, u - RS + 1)
        slot = load.turn % RS
        load.turn += 1
        dst = raw[:, slot, :]
        if len(src.shape) == 3:
            dst = dst.rearrange("p (k c) -> p k c", c=P)
        sp.dma_start(dst, src).then_inc(raw_landed[slot], 16)

    load.turn = 0
    split_done = sem("split_done")
    raw_landed = [sem(f"raw_landed{i}") for i in range(RS)]

    def used(u, c=None):
        for L in range(2):
            v = u - U_MEM[L]
            if 0 <= v < 3 * NMP:
                p = v // 3 + NMP * L
                return (sem("mem_v_proj"), p + 1) if v % 3 == 2 else (sem("mem_qk_proj"), 3 * p + (3, 1)[v % 3])
            v = u - U_OUT[L]
            if 0 <= v < KT:
                return go[L]("product", 16 * (v // 2 + 1))
            v = u - U_FFN[L]
            if 0 <= v < 6 * NCH:
                c, j = (v // 6, v % 6) if c is None else (c, v)
                if j < 4:
                    return gf[L]("up", 4 * c + 3 + j // 2)
                return gf[L]("product", 16 * (c + 1))
        v = u - U_DIL
        if 0 <= v < 3 * NDP:
            p = v // 3
            return (sem("dil_v_proj"), 2 * p + 2) if v % 3 == 2 else (sem("dil_qk_proj"), 4 * p + 2 + 2 * (v % 3))
        if u < U_U:
            return sem("vproj_product"), NT * ((u - U_V) // 2 + 1)
        return sem("uproj_product"), NT * ((u - U_U) // 2 + 1)

    def slot_of(u):
        if u < U_OUT[0]:
            return u % 3
        if u < U_MEM[1]:
            return u % WS
        return [2, 3, 4, 0, 1, 2][u - U_MEM[1]] if u < U_V else (u - U_V) % WS

    def user_before(u):
        return max((v for v in range(u) if slot_of(v) == slot_of(u)), default=None)

    def split(pool, u, before=None, turn=None, rounds=None, slot=None):
        if slot is None:
            slot = slot_of(u)
            before = user_before(u) if before is None else before
        turn = u % RS if turn is None else turn
        pool.wait_ge(raw_landed[turn], 16 * (u // RS + 1) if rounds is None else 16 * rounds)
        if before is not None:
            pool.wait_ge(*(before if isinstance(before, tuple) else used(before)))
        nc.gpsimd.tensor_tensor(Wh[:, slot, :], raw[:, turn, :], zcol[:, 0:1].to_broadcast([P, UNIT]),
                                ALU.add).then_inc(high_done, 1)
        pool.wait_ge(high_done, u + 1)
        nc.gpsimd.tensor_tensor(Wl[:, slot, :], raw[:, turn, :], Wh[:, slot, :].bitcast(F32),
                                ALU.subtract).then_inc(split_done, 1)

    high_done = sem("high_done")

    def three(dst, wh, wl, xh, xl, first, last):
        nc.tensor.matmul(dst, wh, xh, start=first, stop=False)
        nc.tensor.matmul(dst, wh, xl, start=False, stop=False)
        return nc.tensor.matmul(dst, wl, xh, start=False, stop=last)

    def wtile(slot, k):
        return Wh[:, slot, k * P:(k + 1) * P], Wl[:, slot, k * P:(k + 1) * P]

    def rows_in(dst, slot, xh, xl, lo, n):
        for k in range(KT):
            wh, wl = wtile(slot, k)
            mm = three(dst, wh, wl, xh[:, k, lo:lo + n], xl[:, k, lo:lo + n], k == 0, k == KT - 1)
        return mm

    def tile_of(n):
        return 2 * (n // 4) + n % 2, (n // 2) % 2

    def width(kind, n):
        return M if kind == "mem" else P * (tile_of(n)[0] + 1)

    def keytiles(kind, s):
        return 2 if kind == "mem" else 2 * (s // 2) + 2

    def items(kind):
        found = []
        for s in range(8):
            nk = keytiles(kind, s)
            for lo in range(0, nk, 4):
                found.append((s, lo, min(4, nk - lo), lo == 0, lo + 4 >= nk))
        return found

    def item_of(kind, s):
        return max(i for i, it in enumerate(items(kind)) if it[0] == s)

    def blocks(kind, it, i):
        s, lo, nk, _, last = it
        return nk - 1 if kind == "dil" and last and i == 0 else nk

    def pair_names(kind):
        def g(name, value=None):
            s = sem(f"{kind}_{name}")
            return s if value is None else (s, value)
        return g

    def qk_groups(kind):
        if kind == "mem":
            return [("k", 0, 2), ("q", 0, 0), ("q", 1, 1)]
        return [("q", 0, 0), ("q", 1, 1), ("k", 0, 2), ("k", 1, 3)]

    def s_view(kind, n):
        w, b = width(kind, n), 2 * (n % 2)
        if w > 512:
            return ps[:, 512 * b:512 * b + 1024].rearrange("p (a c) -> p a c", c=512)[:, :, 0:w // 2]
        return bank(b, w)

    def qk_pe(pe, kind, j, u, slots):
        what, h, b = qk_groups(kind)[j]
        un = "qk".index(what)
        pe.wait_ge(split_done, u + un + 1)
        if what == "k" and kind == "mem":
            mm = rows_in(bank(b, M), slots[un], memTh, memTl, 0, M)
        else:
            mm = rows_in(bank(b), slots[un], XTh, XTl, h * 512, 512)
        mm.then_inc(sem(f"{kind}_qk_proj"), 1)

    def qk_act(act, kind, pi, j):
        g = pair_names(kind)
        bf = MemBuf if kind == "mem" else DilBuf
        what, h, b = qk_groups(kind)[j]
        act.wait_ge(*g("qk_proj", pi * len(qk_groups(kind)) + j + 1))
        if what == "q":
            for hd in range(2):
                r = slice(HD * hd, HD * hd + HD)
                nc.scalar.activation(bf.Qh[r, hd, h * 512:h * 512 + 512], bank(b)[r, :], ACT.Copy,
                                     scale=QSCALE).then_inc(g("q_high"), 1)
        else:
            n = M if kind == "mem" else 512
            nc.scalar.activation(Kh[:, h * 512:h * 512 + n], bank(b, n), ACT.Copy).then_inc(g("k_high"), 1)

    def qk_dve(dve, kind, pi, j):
        g = pair_names(kind)
        bf = MemBuf if kind == "mem" else DilBuf
        what, h, b = qk_groups(kind)[j]
        if what == "q":
            for hd in range(2):
                dve.wait_ge(*g("q_high", pi * 4 + 2 * h + hd + 1))
                r = slice(HD * hd, HD * hd + HD)
                cs = slice(h * 512, h * 512 + 512)
                nc.vector.scalar_tensor_tensor(bf.Ql[r, hd, cs], bank(b)[r, :], QSCALE,
                                               bf.Qh[r, hd, cs].bitcast(F32), ALU.mult,
                                               ALU.subtract).then_inc(g("q_low"), 1)
        else:
            n, nh = (M, 1) if kind == "mem" else (512, 2)
            dve.wait_ge(*g("k_high", pi * nh + h + 1))
            cs = slice(h * 512, h * 512 + n)
            nc.vector.tensor_tensor(Kl[:, cs], bank(b, n), Kh[:, cs].bitcast(F32), ALU.subtract).then_inc(g("k_low"), 1)

    def pair_pe(pe, kind, pi, u, slots, fill):
        g = pair_names(kind)
        bf = MemBuf if kind == "mem" else DilBuf
        Kn = M if kind == "mem" else S
        nh = 1 if kind == "mem" else 2
        its = items(kind)
        NI = len(its)

        def scores(n):
            qt, hd = tile_of(n)
            w = width(kind, n)
            if n >= 2:
                pe.wait_ge(*g("logits", pi * 16 + n - 1))
            nb = max(256, w) if w <= 512 else w // 2
            for i in range(1 if w <= 512 else 2):
                dst = bank(2 * (n % 2) + i, nb)
                ks = slice(i * nb, (i + 1) * nb)
                q0 = slice(qt * P, (qt + 1) * P)
                mm = three(dst, bf.Qh[:, hd, q0], bf.Ql[:, hd, q0], Kh[:, ks], Kl[:, ks], True, True)
            mm.then_inc(g("scores"), 1)

        def turn(i, ab):
            s, lo, nk, first, last = its[i]
            if first:
                pe.wait_ge(*g("probs", pi * 16 + 2 * s + ab + 1))
            if i >= 1:
                pe.wait_ge(*g("pt_low", pi * 2 * NI + 2 * (i - 1) + ab + 1))
            for k in range(blocks(kind, its[i], ab)):
                mm = nc.tensor.transpose(bank(4 + ab, P, k * P),
                                         bf.Pb[:, (2 * s + ab) % 3, (lo + k) * P:(lo + k + 1) * P], ident[:, :])
            mm.then_inc(g("turned"), 1)

        def pv(i):
            s, lo, nk, first, last = its[i]
            c, hd = s // 2, s % 2
            pe.wait_ge(*g("pt_low", pi * 2 * NI + 2 * i + 2))
            if i == 0:
                pe.wait_ge(*g("v_low", (pi + 1) * nh))
            if kind == "dil" and last:
                pe.wait_ge(*g("pt_zero", (pi * 8 + s + 1) * 2))
            if hd == 0 and first and c >= 2:
                pe.wait_ge(*g("mixed", pi * 4 + c))
            dst = bank(6 + c % 2, 2 * P)
            for k in range(nk):
                mm = three(dst, bf.Vh[:, lo + k, HD * hd:HD * hd + P], bf.Vl[:, lo + k, HD * hd:HD * hd + P],
                           PTh[:, i % 2, k, :, :], PTl[:, i % 2, k, :, :],
                           hd == 0 and first and k == 0, hd == 1 and last and k == nk - 1)
            mm.then_inc(g("pv"), 1)
            if hd == 1 and last:
                pe.wait_ge(*g("rden_wide", pi * 4 + c + 1))
                for q in range(2):
                    mm = nc.tensor.transpose(bank(6 + c % 2, P, 256 + q * P),
                                             bf.RB[:, q, :, :].rearrange("p a d -> p (a d)"), ident[:, :])
                mm.then_inc(g("rden_turned"), 1)

        def values(h):
            if h == 0:
                pe.wait_ge(split_done, u + 3)
            if kind == "mem":
                mm = rows_in(bank(4, M), slots[2], memTh, memTl, 0, M)
            else:
                mm = rows_in(bank(4 + h), slots[2], XTh, XTl, h * 512, 512)
            mm.then_inc(g("v_proj"), 1)

        pe.wait_ge(*g("mixed", pi * 4 + 1))
        values(0)
        pe.wait_ge(*g("k_low", (pi + 1) * nh))
        pe.wait_ge(*g("q_low", (pi + 1) * 4))
        scores(0)
        if nh == 2:
            values(1)
        scores(1)
        pe.wait_ge(*g("v_copied", (pi + 1) * nh))
        for t in range(Kn // P):
            mm = nc.tensor.transpose(bank(6 + t // 4, P, (t % 4) * P), bf.vT[:, t * P:(t + 1) * P], ident[:, :])
            if t % 4 == 3 or t == Kn // P - 1:
                mm.then_inc(g("v_turned"), 1)
        for i, (s, lo, nk, first, last) in enumerate(its):
            if first and s < 7:
                scores(2 * s + 2)
                if last:
                    scores(2 * s + 3)
            turn(i, 0)
            turn(i, 1)
            if first and not last and s < 7:
                scores(2 * s + 3)
            if i >= 1:
                pv(i - 1)
        if fill:
            fill[0]()
        pv(NI - 1)
        for f in fill[1:]:
            f()

    def pair_act(act, kind, pi, fill, beside=lambda i: None):
        g = pair_names(kind)
        bf = MemBuf if kind == "mem" else DilBuf
        Kn = M if kind == "mem" else S
        nh = 1 if kind == "mem" else 2
        its = items(kind)
        NI = len(its)

        def v_copy(h):
            act.wait_ge(*g("v_proj", pi * nh + h + 1))
            n = min(512, Kn)
            nc.scalar.activation(bf.vT[:, h * 512:h * 512 + n], bank(4 + h, n), ACT.Copy).then_inc(g("v_copied"), 1)

        def v_high(j):
            act.wait_ge(*g("v_turned", pi * nh + j + 1))
            m = min(4, Kn // P)
            src = bank(6 + j, m * P).rearrange("p (t a d) -> p t a d", a=2, d=HD)
            for hd in range(2):
                nc.scalar.activation(bf.Vh[:, 4 * j:4 * j + m, 2 * HD * hd:2 * HD * hd + HD],
                                     src[:, :, hd, :], ACT.Copy).then_inc(g("v_high"), 1)

        def exp(n):
            act.wait_ge(*g("logits", pi * 16 + n + 1))
            p = bf.Pb[:, n % 3, 0:width(kind, n)]
            nc.scalar.activation(p, p, ACT.Exp, bias=mneg[:, n:n + 1], scale=-1.0,
                                 accum_out=den[:, n:n + 1]).then_inc(g("probs"), 1)

        def pt_high(i, ab):
            act.wait_ge(*g("turned", pi * 2 * NI + 2 * i + ab + 1))
            if i >= 2:
                act.wait_ge(*g("pv", pi * NI + i - 1))
            k = blocks(kind, its[i], ab)
            if k:
                nc.scalar.activation(PTh[:, i % 2, 0:k, ab, :], bank(4 + ab, k * P).rearrange("p (k q) -> p k q", q=P),
                                     ACT.Copy).then_inc(g("pt_high"), 1)

        def rden_copy(c):
            act.wait_ge(*g("rden_turned", pi * 4 + c + 1))
            nc.scalar.activation(bf.RSb[:, :], bank(6 + c % 2, 256, 256), ACT.Copy).then_inc(g("rden_copied"), 1)

        v_copy(0)
        exp(0)
        if nh == 2:
            v_copy(1)
        exp(1)
        for j in range(nh):
            v_high(j)
        for i, (s, lo, nk, first, last) in enumerate(its):
            pt_high(i, 0)
            if first and last and s < 7:
                exp(2 * s + 2)
            pt_high(i, 1)
            if first and not last and s < 7:
                exp(2 * s + 2)
            if last and s < 7:
                exp(2 * s + 3)
            if last and s % 2 == 0 and s >= 2:
                rden_copy(s // 2 - 1)
            beside(i)
        if fill:
            fill[0]()
        rden_copy(3)
        for f in fill[1:]:
            f()

    def pair_dve(dve, kind, pi, dst, fill, beside=lambda i: None):
        g = pair_names(kind)
        bf = MemBuf if kind == "mem" else DilBuf
        nh = 1 if kind == "mem" else 2
        its = items(kind)
        NI = len(its)

        def v_low(j):
            dve.wait_ge(*g("v_high", (pi * nh + j + 1) * 2))
            m = 2 if kind == "mem" else 4
            src = bank(6 + j, m * P).rearrange("p (t a d) -> p t a d", a=2, d=HD)
            for hd in range(2):
                vs = (slice(None), slice(4 * j, 4 * j + m), slice(2 * HD * hd, 2 * HD * hd + HD))
                ins = nc.vector.tensor_tensor(bf.Vl[vs], src[:, :, hd, :], bf.Vh[vs].bitcast(F32), ALU.subtract)
            ins.then_inc(g("v_low"), 1)

        def logits(n):
            qt, hd = tile_of(n)
            w = width(kind, n)
            dve.wait_ge(*g("scores", pi * 16 + n + 1))
            if n == 2:
                dve.wait_ge(*g("v_turned", (pi + 1) * nh))
            if n >= 3:
                dve.wait_ge(*g("turned", pi * 2 * NI + 2 * item_of(kind, (n - 3) // 2) + (n - 3) % 2 + 1))
            if kind == "dil":
                if n == 0 or n == 2:
                    dve.wait_ge(*g(f"bias_landed{hd}", (pi + 1) * 16))
                bias = bf.B[:, hd, S - P - qt * P:S - P - qt * P + w]
            else:
                bias = bf.zero[:, :]
            nc.vector.memset(tick[:, n:n + 1], 0.0)
            o = bf.Pb[:, n % 3, 0:w]
            if w > 512:
                bias = bias.rearrange("p (a c) -> p a c", a=2)
                o = o.rearrange("p (a c) -> p a c", a=2)
            nc.vector.tensor_tensor_reduce(o, s_view(kind, n), bias, -1.0, 3e38, ALU.add, ALU.min,
                                           mneg[:, n:n + 1]).then_inc(g("logits"), 1)

        def pt_low(i, ab):
            dve.wait_ge(*g("pt_high", pi * 2 * NI + 2 * i + ab + 1))
            k = blocks(kind, its[i], ab)
            nc.vector.tensor_tensor(PTl[:, i % 2, 0:k, ab, :], bank(4 + ab, k * P).rearrange("p (k q) -> p k q", q=P),
                                    PTh[:, i % 2, 0:k, ab, :].bitcast(F32), ALU.subtract).then_inc(g("pt_low"), 1)

        def zero(i):
            if i >= 2:
                dve.wait_ge(*g("pv", pi * NI + i - 1))
            k = its[i][2] - 1
            nc.vector.memset(PTh[:, i % 2, k, 0, :].bitcast(F32), 0.0).then_inc(g("pt_zero"), 1)
            nc.vector.memset(PTl[:, i % 2, k, 0, :].bitcast(F32), 0.0).then_inc(g("pt_zero"), 1)

        def rden_of(c):
            t0 = 4 * c
            dve.wait_ge(*g("probs", pi * 16 + t0 + 4))
            if c >= 1:
                dve.wait_ge(*g("rden_turned", pi * 4 + c))
            nc.vector.reciprocal(rden[:, t0:t0 + 4], den[:, t0:t0 + 4]).then_inc(g("rden"), 1)
            dve.wait_ge(*g("rden", pi * 4 + c + 1))
            src = rden[:, t0:t0 + 4].rearrange("p (h i) -> p i h", h=2).unsqueeze(3).to_broadcast([P, 2, 2, HD])
            nc.vector.tensor_copy(bf.RB[:, :, :, :], src).then_inc(g("rden_wide"), 1)

        def mix(c):
            dve.wait_ge(*g("rden_copied", pi * 4 + c + 1))
            nc.vector.tensor_tensor(dst(pi, c), bank(6 + c % 2, 256), bf.RSb[:, :], ALU.mult).then_inc(g("mixed"), 1)

        logits(0)
        logits(1)
        for j in range(nh):
            v_low(j)
        for i, (s, lo, nk, first, last) in enumerate(its):
            if first and s < 7:
                logits(2 * s + 2)
            if last and kind == "dil":
                zero(i)
            pt_low(i, 0)
            if last and s < 7:
                logits(2 * s + 3)
            pt_low(i, 1)
            if last and s % 2 == 0 and s >= 2:
                mix(s // 2 - 1)
            if last and s % 2 == 1:
                rden_of(s // 2)
            beside(i)
        if fill:
            fill[0]()
        mix(3)
        for f in fill[1:]:
            f()

    def fills(make, kind):
        return [lambda j=j: make(j) for j in range(len(qk_groups(kind)))]

    def mem_dst(pi, c):
        return MO[:, pi % NMP, c * 256:(c + 1) * 256]

    def dil_dst(pi, c):
        return mixT[:, bass.ds(pi, 1), c * 256:(c + 1) * 256].rearrange("p a c -> p (a c)")

    def turn_pe(pe, g, t, src, nk=KT, bb=0):
        if t >= 2:
            pe.wait_ge(*g("xt_low", t - 1))
        b = bb + 2 * (t % 2)
        for k in range(nk):
            mm = nc.tensor.transpose(bank(b + k // 4, P, (k % 4) * P), src[:, k * P:(k + 1) * P], ident[:, :])
        mm.then_inc(g("xt_turned"), 1)

    def turned(t, nk, bb):
        b = bb + 2 * (t % 2)
        return ps[:, 512 * b:512 * b + nk * P].rearrange("p (k q) -> p k q", q=P)

    def turn_act(act, g, t, nk=KT, bb=0, high=XTh):
        act.wait_ge(*g("xt_turned", t + 1))
        nc.scalar.activation(high[:, 0:nk, t * P:(t + 1) * P], turned(t, nk, bb), ACT.Copy).then_inc(g("xt_high"), 1)

    def turn_dve(dve, g, t, nk=KT, bb=0, high=XTh, low=XTl):
        dve.wait_ge(*g("xt_high", t + 1))
        nc.vector.tensor_tensor(low[:, 0:nk, t * P:(t + 1) * P], turned(t, nk, bb),
                                high[:, 0:nk, t * P:(t + 1) * P].bitcast(F32), ALU.subtract).then_inc(g("xt_low"), 1)

    def acc_pe(pe, g, c, u, lhs, slots, ready, after=None):
        pe.wait_ge(split_done, u + 2)
        for t in range(NT):
            ready(t)
            for h in range(2):
                n = 2 * t + h
                if not (isinstance(c, int) and c * 16 + n < 4):
                    pe.wait_ge(*g("added", c * 16 + n - 3 + g.credit))
                for k in range(2):
                    lh, ll = lhs(k, t)
                    mm = three(bank(4 + n % 4), lh, ll, Wh[:, slots[k], h * 512:(h + 1) * 512],
                               Wl[:, slots[k], h * 512:(h + 1) * 512], k == 0, k == 1)
                mm.then_inc(g("product"), 1)
            if after:
                after(t)

    def acc_dve(dve, g, c, t, scaled=None):
        for h in range(2):
            n = 2 * t + h
            dve.wait_ge(*g("product", c * 16 + n + 1))
            x = XR[:, t, h * 512:(h + 1) * 512]
            if scaled:
                nc.vector.scalar_tensor_tensor(x, x, scaled, bank(4 + n % 4), ALU.mult, ALU.add).then_inc(g("added"), 1)
            else:
                nc.vector.tensor_tensor(x, x, bank(4 + n % 4), ALU.add).then_inc(g("added"), 1)

    SKEW = 3

    def norm_pe_after(pe, g):
        def after(t):
            if SKEW <= t < SKEW + 4:
                pe.wait_ge(*g("shifted", t - SKEW + 1))
                turn_pe(pe, g, t - SKEW, XR[:, t - SKEW, :])
        return after

    def late_turn(pe, g, q, c):
        if q == 4:
            pe.wait_ge(*g("added", c * 16 + 16 + g.credit))
        pe.wait_ge(*g("shifted", q + 1))
        turn_pe(pe, g, q, XR[:, q, :], bb=4)

    def norm_dve(dve, g, c, last, beside=lambda q: None):
        nself = 0
        for t in range(NT + SKEW):
            if t < NT:
                acc_dve(dve, g, c, t)
                dve.wait_ge(*g("added", c * 16 + 2 * t + 2 + g.credit))
                for h in range(2):
                    nc.vector.bn_stats(st[:, t, h, :], XR[:, t, h * 512:(h + 1) * 512]).then_inc(g("ln_self"), 1)
                nself += 2
                dve.wait_ge(*g("ln_self", nself))
                nc.vector.bn_aggr(mv[:, t, :], st[:, t, 0:2, :].rearrange("p a b -> p (a b)")).then_inc(g("stats"), 1)
            if 1 <= t <= NT:
                q = t - 1
                dve.wait_ge(*g("root", t))
                nc.vector.reciprocal(rstd[:, q:q + 1], rstd[:, q:q + 1]).then_inc(g("ln_self"), 1)
                nself += 1
                dve.wait_ge(*g("ln_self", nself))
                nc.vector.tensor_scalar(nmr[:, q:q + 1], mv[:, q, 0:1], rstd[:, q:q + 1], -1.0, ALU.mult,
                                        ALU.mult).then_inc(g("rstd"), 1)
            if t >= SKEW and not last:
                turn_dve(dve, g, t - SKEW, bb=4 * (t - SKEW >= 4))
                beside(t - SKEW)

    def norm_act(act, g, last, beside=lambda q: None):
        for t in range(NT + SKEW):
            if t < NT:
                act.wait_ge(*g("stats", t + 1))
                nc.scalar.activation(rstd[:, t:t + 1], mv[:, t, 1:2], ACT.Sqrt, bias=eps[:, 0:1]).then_inc(g("root"), 1)
            if 1 <= t <= NT:
                q = t - 1
                act.wait_ge(*g("rstd", t))
                nc.scalar.activation(XR[:, q, :], XR[:, q, :], ACT.Identity, bias=nmr[:, q:q + 1],
                                     scale=rstd[:, q:q + 1]).then_inc(g("normed"), 1)
            if t >= SKEW and not last:
                turn_act(act, g, t - SKEW, bb=4 * (t - SKEW >= 4))
                beside(t - SKEW)

    def norm_pool(pool, g):
        pool.wait_ge(*g("gb_landed", 32))
        for t in range(NT):
            pool.wait_ge(*g("normed", t + 1))
            nc.gpsimd.tensor_tensor(XR[:, t, :], XR[:, t, :], gb[:, 0, :], ALU.mult).then_inc(g("gained"), 1)
            pool.wait_ge(*g("gained", t + 1))
            nc.gpsimd.tensor_tensor(XR[:, t, :], XR[:, t, :], gb[:, 1, :], ALU.add).then_inc(g("shifted"), 1)

    def load_gb(eng, g, gain, shift, dst):
        n = dst.shape[2]
        for i, w in enumerate((gain, shift)):
            eng.dma_start(dst[:, i, :], w.rearrange("(a n) -> a n", a=1).to_broadcast([P, n])).then_inc(g("gb_landed"), 16)

    class Names:
        def __init__(self, phase, rises=(), layer=0, credit=0):
            self.phase, self.rises, self.layer, self.credit = phase, dict(rises), layer, credit

        def __call__(self, name, value=None):
            s = sem(f"{self.phase}_{name}")
            return s if value is None else (s, value + self.layer * self.rises.get(name, 0))

    NORM = {"xt_turned": NT, "xt_high": NT, "xt_low": NT, "stats": NT, "root": NT, "rstd": NT, "normed": NT,
            "gained": NT, "shifted": NT, "ln_self": 3 * NT, "gb_landed": 32}
    OUT = {**NORM, "product": 16 * KT // 2, "added": 16 * KT // 2}
    FFN = {**NORM, "product": 16 * NCH, "added": 16 * NCH,
           **{x: 4 * NCH for x in ("gate", "up", "silu", "gated", "hid_high", "hid_low")}}
    gi = Names("in")
    gm = [Names("memory", {"xt_turned": 2, "xt_high": 2, "xt_low": 2}, L) for L in range(2)]
    go = [Names("out", OUT, L) for L in range(2)]
    gf = [Names("ffn", FFN, L, 4) for L in range(2)]

    def ffn_slots(L):
        return [slot_of(U_FFN[L] + j) for j in range(6)]

    def ffn_pe(pe, L, c, first, last):
        g = gf[L]
        sl = ffn_slots(L)
        u = U_FFN[L] + c * 6
        if first:
            pe.wait_ge(*go[L]("xt_low", 4))
        for h in range(2):
            if first and h == 1:
                pe.wait_ge(*go[L]("xt_low", NT))
            for m in range(2):
                i = 2 * h + m
                if h == 0:
                    pe.wait_ge(split_done, u + 2 * m + 2)
                pe.wait_ge(*g("gated", c * 4 + i - 2 + 1 + 2))
                for j, name in enumerate(("gate", "up")):
                    rows_in(bank(2 * (i % 2) + j), sl[2 * m + j], XTh, XTl, h * 512, 512).then_inc(g(name), 1)
                    if first and h == 0:
                        late_turn(pe, go[L], 4 + 2 * m + j, KT // 2 - 1)

        def ready(t):
            if t % 4 == 0:
                pe.wait_ge(*g("hid_low", c * 4 + 2 * (t // 4) + 2 + 2))

        acc_pe(pe, g, c, u + 4, lambda k, t: (hidh[:, k, t * P:(t + 1) * P], hidl[:, k, t * P:(t + 1) * P]),
               sl[4:6], ready, after=norm_pe_after(pe, g) if last and L == 0 else None)

    def ffn_silu(act, L, c, i):
        g = gf[L]
        act.wait_ge(*g("gate", c * 4 + i + 1))
        act.wait_ge(*g("gated", c * 4 + i - 2 + 1 + 2))
        nc.scalar.activation(silu[:, i % 2, :], bank(2 * (i % 2)), ACT.Silu).then_inc(g("silu"), 1)

    def ffn_high(act, L, c, i):
        g = gf[L]
        h, m = i // 2, i % 2
        act.wait_ge(*g("gated", c * 4 + i + 1 + 2))
        nc.scalar.activation(hidh[:, m, h * 512:(h + 1) * 512], hid[:, i % 2, :], ACT.Copy).then_inc(g("hid_high"), 1)

    def ffn_gated(dve, L, c, i):
        g = gf[L]
        dve.wait_ge(*g("silu", c * 4 + i + 1))
        dve.wait_ge(*g("up", c * 4 + i + 1))
        dve.wait_ge(*g("hid_low", c * 4 + i - 2 + 1 + 2))
        nc.vector.tensor_tensor(hid[:, i % 2, :], silu[:, i % 2, :], bank(2 * (i % 2) + 1),
                                ALU.mult).then_inc(g("gated"), 1)

    def ffn_low(dve, L, c, i):
        g = gf[L]
        h, m = i // 2, i % 2
        dve.wait_ge(*g("hid_high", c * 4 + i + 1))
        nc.vector.tensor_tensor(hidl[:, m, h * 512:(h + 1) * 512], hid[:, i % 2, :],
                                hidh[:, m, h * 512:(h + 1) * 512].bitcast(F32),
                                ALU.subtract).then_inc(g("hid_low"), 1)

    def ffn_beside(one, two, L):
        def beside(q):
            if q == 5:
                one(0)
            elif q == 6:
                two(0)
            elif q == 7:
                one(1)
                two(1)
                for i in (2, 3):
                    one(i)
                    two(i)
        return beside

    gvp, gup, gsg = Names("vproj"), Names("uproj"), Names("sgu")

    def wide_pe(pe, g, u, n):
        j, t = n // NT, n % NT
        if t == 0:
            pe.wait_ge(split_done, u + 2 * j + 2)
        if n >= 4:
            pe.wait_ge(*g("gelu", n - 3))
        s0 = slot_of(u + 2 * j)
        dst = bank(n % 4, M).rearrange("p (a c) -> p a c", c=P)
        for k in range(KT):
            mm = three(dst, XTh[:, k, t * P:(t + 1) * P], XTl[:, k, t * P:(t + 1) * P],
                       Wh[:, s0:s0 + 2, k * P:(k + 1) * P], Wl[:, s0:s0 + 2, k * P:(k + 1) * P],
                       k == 0, k == KT - 1)
        mm.then_inc(g("product"), 1)

    def channels(n):
        return V[:, n % NT, (n // NT) * M:(n // NT + 1) * M]

    MIX_AT = {3: (0, 1, 2, 3), 4: (4, 5), 5: (6, 7), 6: (8, 9), 7: (10, 11)}

    def turn_ws(pe):
        pe.wait_ge(*gsg("lower", 1))
        for i in range(NG):
            mm = nc.tensor.transpose(bank(4 + i // 4, P, (i % 4) * P), wsraw[:, i, :], ident[:, :])
        mm.then_inc(gsg("ws_turned"), 1)

    def sgu_pe(pe):
        for n in range(3 * NT):
            wide_pe(pe, gvp, U_V, n)
            if n == 8:
                turn_ws(pe)
        for n in range(3 * NT):
            wide_pe(pe, gup, U_U, n)
            if n in MIX_AT:
                pe.wait_ge(*gsg("ws_low", 1))
            for i in MIX_AT.get(n, ()):
                pe.wait_ge(*gsg("v_low", i + 1))
                if i >= 4:
                    pe.wait_ge(*gsg("gate", i - 3))
                three(bank(4 + i % 4), WSh[:, i, :], WSl[:, i, :],
                      VSh[:, i % 2, :, :].rearrange("p a b -> p (a b)"),
                      VSl[:, i % 2, :, :].rearrange("p a b -> p (a b)"), True, True).then_inc(gsg("spatial"), 1)
            t = n - 2 * NT - 1
            if t >= 0:
                sgu_turn(pe, t)
        sgu_turn(pe, NT - 1)

    def sgu_turn(pe, t):
        pe.wait_ge(*gsg("gate", NG))
        pe.wait_ge(*gup("gated", 2 * NT + t + 1))
        turn_pe(pe, gup, t, V[:, t, :], DIL_W // P, 4)

    def sgu_act(act):
        act.wait_ge(sem("mem_mixed"), 8 * NMP + 1)
        act.dma_start(wsraw[:, :, :], a["sgu_w_s"][0].rearrange("g t s -> t g s")).then_inc(gsg("ws_landed"), 16)
        with nc.allow_non_contiguous_dma(reason="1536 biases, once"):
            act.dma_start(bst[:, :], a["sgu_b_s"][0].rearrange("g t -> t g")).then_inc(gsg("bs_landed"), 16)

        for n in range(3 * NT):
            act.wait_ge(*gvp("product", n + 1))
            nc.scalar.activation(channels(n), bank(n % 4, M), ACT.Gelu_apprx_tanh).then_inc(gvp("gelu"), 1)
            if n == 9:
                act.wait_ge(*gsg("ws_turned", 1))
                nc.scalar.activation(WSh[:, :, :], ps[:, 2048:2048 + NG * P].rearrange("p (g t) -> p g t", t=P),
                                     ACT.Copy).then_inc(gsg("ws_high"), 1)
                load_gb(act, gsg, a["sgu_ln_g"][0], a["sgu_ln_b"][0], sgb)
            if n >= 2 * NT and n % 4 == 3:
                t0 = n % NT - 3
                act.wait_ge(*gsg("stats", t0 + 4))
                nc.scalar.activation(rstd[:, t0:t0 + 4], mv[:, t0:t0 + 4, 1], ACT.Sqrt,
                                     bias=eps[:, 0:1]).then_inc(gsg("root"), 1)

        def gelu(n):
            act.wait_ge(*gup("product", n + 1))
            if n >= 2:
                act.wait_ge(*gup("gated", n - 1))
            nc.scalar.activation(ub[:, n % 2, :], bank(n % 4, M), ACT.Gelu_apprx_tanh).then_inc(gup("gelu"), 1)

        gelu(0)
        gelu(1)
        for n in sorted(MIX_AT):
            for i in MIX_AT[n]:
                if i == 0:
                    act.wait_ge(*gsg("shifted", NT))
                if i >= 2:
                    act.wait_ge(*gsg("spatial", i - 1))
                nc.scalar.activation(VSh[:, i % 2, :, :], V[:, :, i * HD:(i + 1) * HD], ACT.Copy
                                     ).then_inc(gsg("v_high"), 1)
            gelu(n - 1)
        act.wait_ge(*gsg("spatial", NG))
        load_gb(act, go[1], a["ln_mix_g"][1], a["ln_mix_b"][1], gb)

        def turn(t):
            ts = slice(t * P, (t + 1) * P)
            turn_act(act, gup, t, DIL_W // P, 4)
            nc.scalar.activation(XTh[:, 6:8, ts], MO[:, :, ts], ACT.Copy).then_inc(gup("mo_high"), 1)

        for n in range(7, 3 * NT):
            gelu(n)
            if n >= 2 * NT + 2:
                turn(n - 2 * NT - 2)
        turn(NT - 2)
        turn(NT - 1)

    def sgu_dve(dve):
        for n in range(3 * NT):
            j, t = n // NT, n % NT
            dve.wait_ge(*gvp("gelu", n + 1))
            nc.vector.bn_stats(st[:, t, j, :], channels(n)).then_inc(gsg("partial"), 1)
            if n == 10:
                dve.wait_ge(*gsg("ws_high", 1))
                nc.vector.tensor_tensor(WSl[:, :, :], ps[:, 2048:2048 + NG * P].rearrange("p (g t) -> p g t", t=P),
                                        WSh[:, :, :].bitcast(F32), ALU.subtract).then_inc(gsg("ws_low"), 1)
            if j == 2:
                dve.wait_ge(*gsg("partial", n + 1))
                nc.vector.bn_aggr(mv[:, t, :], st[:, t, :, :].rearrange("p a b -> p (a b)")).then_inc(gsg("stats"), 1)
                if t % 4 == 3:
                    t0 = t - 3
                    dve.wait_ge(*gsg("root", t // 4 + 1))
                    nc.vector.reciprocal(rstd[:, t0:t0 + 4], rstd[:, t0:t0 + 4]).then_inc(gsg("rstd"), 1)
                    dve.wait_ge(*gsg("rstd", t // 4 + 1))
                    dve.wait_ge(*gsg("gb_landed", 32))
                    for q in range(t0, t0 + 4):
                        nc.vector.tensor_scalar(V[:, q, :], V[:, q, :], mv[:, q, 0:1], rstd[:, q:q + 1], ALU.subtract,
                                                ALU.mult).then_inc(gsg("normed"), 1)
                        dve.wait_ge(*gsg("normed", q + 1))
                        nc.vector.tensor_tensor(V[:, q, :], V[:, q, :], sgb[:, 0, :], ALU.mult).then_inc(gsg("gained"), 1)
        dve.wait_ge(*gsg("bs_landed", 16))

        def gate(i):
            dve.wait_ge(*gsg("spatial", i + 1))
            nc.vector.tensor_scalar(V[:, :, i * HD:(i + 1) * HD], bank(4 + i % 4).rearrange("p (t c) -> p t c", c=HD),
                                    bst[:, i:i + 1], None, ALU.add).then_inc(gsg("gate"), 1)

        def gated(n):
            dve.wait_ge(*gup("gelu", n + 1))
            dve.wait_ge(*gsg("gate", 4 * (n // NT) + 4))
            nc.vector.tensor_tensor(channels(n), channels(n), ub[:, n % 2, :], ALU.mult).then_inc(gup("gated"), 1)

        for n in sorted(MIX_AT):
            for i in MIX_AT[n]:
                dve.wait_ge(*gsg("v_high", i + 1))
                nc.vector.tensor_tensor(VSl[:, i % 2, :, :], V[:, :, i * HD:(i + 1) * HD],
                                        VSh[:, i % 2, :, :].bitcast(F32), ALU.subtract).then_inc(gsg("v_low"), 1)
                if i != MIX_AT[n][0]:
                    gate(i - 1)
            gate(MIX_AT[n][-1])
            if n == 3:
                gated(0)
            gated(n - 2)

        def turn(t):
            ts = slice(t * P, (t + 1) * P)
            turn_dve(dve, gup, t, DIL_W // P, 4)
            dve.wait_ge(*gup("mo_high", t + 1))
            nc.vector.tensor_tensor(XTl[:, 6:8, ts], MO[:, :, ts], XTh[:, 6:8, ts].bitcast(F32),
                                    ALU.subtract).then_inc(gup("mo_low"), 1)

        for n in range(6, 3 * NT):
            gated(n)
            if n >= 2 * NT + 2:
                turn(n - 2 * NT - 2)
        turn(NT - 2)
        turn(NT - 1)

    def sgu_start(pool):
        pool.wait_ge(*gsg("ws_landed", 16))
        nc.gpsimd.affine_select(out=wsraw[:, :, :], in_=wsraw[:, :, :], compare_op=ALU.is_ge, fill=0.0, base=0,
                                pattern=[[0, NG], [-1, P]], channel_multiplier=1).then_inc(gsg("lower"), 1)

    def sgu_pool(pool):
        for t in range(NT):
            pool.wait_ge(*gsg("gained", t + 1))
            nc.gpsimd.tensor_tensor(V[:, t, :], V[:, t, :], sgb[:, 1, :], ALU.add).then_inc(gsg("shifted"), 1)

    DILSL = [0, 1, 2]
    MIX_ORDER = [0, 1, 2, 3, 4, 6, 7, 5]
    block = nc.Block()
    block.__enter__()

    @block.sync
    def _(sp):
        w = [a["a_w_in"][0], a["b_w_in"][0]]
        mem_q = [3 * DIL_W, 2 * DIL_W]

        def mem_units(L):
            for p in range(NMP):
                u = U_MEM[L] + 3 * p
                load(sp, u, cols(w[L], mem_q[L] + p * P))
                load(sp, u + 1, cols(a["w_mem_kv"][L], p * P))
                load(sp, u + 2, cols(a["w_mem_kv"][L], MEM_W + p * P))

        def out_units(L):
            for k in range(KT):
                if L == 0 and k == 4:
                    for i in range(4):
                        if i == 0:
                            sp.wait_ge(sem("dil_scores"), 16 * NDP)
                        if i == 2:
                            sp.wait_ge(sem("dil_mixed"), 4 * NDP + 1)
                        sp.dma_start(XR[:, 2 * i:2 * i + 2, :],
                                     a["x"][0, 256 * i:256 * i + 256, :].rearrange("(t p) d -> p t d", p=P)
                                     ).then_inc(sem(f"x_again{i}"), 16)
                load(sp, U_OUT[L] + k, a["w_out"][L][k * P:(k + 1) * P, :])

        def ffn_units(L):
            with sp.Fori(0, NCH) as c:
                u = U_FFN[L] + c * 6
                for m in range(2):
                    load(sp, u + 2 * m, cols(a["w_gate"][L], c * 256 + m * P))
                    load(sp, u + 2 * m + 1, cols(a["w_up"][L], c * 256 + m * P))
                for k in range(2):
                    load(sp, u + 4 + k, a["w_down"][L][bass.ds(c * 256 + k * P, P), :])

        mem_units(0)
        for p in range(NDP):
            for j in range(3):
                load(sp, U_DIL + 3 * p + j, cols(w[0], j * DIL_W + p * P))
                if j == 1:
                    for hd in range(2):
                        if p == 0:
                            sp.wait_ge(sem("mem_mixed"), 4 * NMP + 1)
                        else:
                            sp.wait_ge(sem("dil_logits"), 16 * (p - 1) + 14 + 2 * hd)
                        sp.dma_start(DilBuf.B[:, hd, :], a["c_bias"][2 * p + hd]
                                     ).then_inc(sem(f"dil_bias_landed{hd}"), 16)
        out_units(0)
        ffn_units(0)
        mem_units(1)
        for j in range(6):
            load(sp, U_V + j, cols(w[1], DIL_W + j * P))
        for j in range(6):
            load(sp, U_U + j, cols(w[1], j * P))
        out_units(1)
        ffn_units(1)
        for t in range(NT):
            sp.wait_ge(*gf[1]("shifted", t + 1))
            sp.dma_start(out[0, t * P:(t + 1) * P, :], XR[:, t, :]).then_inc(sem("stored"), 16)
        sp.wait_ge(sem("stored"), 16 * NT)

    @block.gpsimd
    def _(pool):
        nc.gpsimd.memset(zcol[:, :], 0.0).then_inc(sem("zcol_set"), 1)
        pool.wait_ge(sem("zcol_set"), 1)
        attention_over = (sem("dil_mixed"), 4 * NDP + 1)
        for u in range(U_FFN[0]):
            split(pool, u, attention_over if U_OUT[0] + 3 <= u < U_OUT[0] + 6 else None)

        def ffn_units(L):
            for j in range(4):
                split(pool, U_FFN[L] + j)
            norm_pool(pool, go[L])
            for j in range(4, 6):
                split(pool, U_FFN[L] + j)
            with pool.Fori(1, NCH) as c:
                for j in range(6):
                    split(pool, U_FFN[L] + c * 6 + j, used(U_FFN[L] + j, c - 1), (U_FFN[L] + j) % RS,
                          U_FFN[L] // 2 + c * 3 + j // 2 + 1, slot_of(U_FFN[L] + j))

        ffn_units(0)
        for j in range(3):
            split(pool, U_MEM[1] + j)
        norm_pool(pool, gf[0])
        for u in range(U_MEM[1] + 3, U_U):
            split(pool, u, (sem("mem_mixed"), 8 * NMP + 1) if U_V + 3 <= u < U_V + 6 else None)
            if u == U_V + 1:
                sgu_start(pool)
        sgu_pool(pool)
        for u in range(U_U, U_FFN[1]):
            split(pool, u)
        ffn_units(1)
        norm_pool(pool, gf[1])

    @block.tensor
    def _(pe):
        pe.wait_ge(sem("const_landed"), 16)
        for t in range(NT):
            if t % 2 == 0:
                pe.wait_ge(sem(f"x_landed{t // 2}"), 16)
            turn_pe(pe, gi, t, XR[:, t, :])
        for t in range(2):
            pe.wait_ge(*gi("xt_low", NT - 1 + t))
            pe.wait_ge(sem("mem_landed0"), 16)
            turn_pe(pe, gm[0], t, memraw[:, t, :])
        for L in range(2):
            def slots(p):
                return [slot_of(U_MEM[L] + 3 * p + j) for j in range(3)]

            def mem_qk(p):
                return fills(lambda j: qk_pe(pe, "mem", j, U_MEM[L] + 3 * p, slots(p)), "mem")

            def dil_qk(p):
                return fills(lambda j: qk_pe(pe, "dil", j, U_DIL + p * 3, DILSL), "dil")

            if L == 0:
                pe.wait_ge(*gi("xt_low", NT))
                pe.wait_ge(*gm[0]("xt_low", 2))
                for f in mem_qk(0):
                    f()
            else:
                for t in range(2):
                    pe.wait_ge(*gf[0]("xt_low", 3 + t))
                    if t == 0:
                        pe.wait_ge(sem("mem_landed1"), 16)
                    turn_pe(pe, gm[1], t, memraw[:, t, :])
                k_, q0, q1 = mem_qk(0)
                late_turn(pe, gf[0], 4, NCH - 1)
                pe.wait_ge(*gm[1]("xt_low", 2))
                k_()
                late_turn(pe, gf[0], 5, NCH - 1)
                q0()
                late_turn(pe, gf[0], 6, NCH - 1)
                late_turn(pe, gf[0], 7, NCH - 1)
                pe.wait_ge(*gf[0]("xt_low", NT))
                q1()
            for p in range(NMP):
                pair_pe(pe, "mem", NMP * L + p, U_MEM[L] + 3 * p, slots(p),
                        mem_qk(p + 1) if p < NMP - 1 else dil_qk(0) if L == 0 else [])
            if L == 0:
                with pe.Fori(0, NDP - 1) as p:
                    pair_pe(pe, "dil", p, p * 3 + U_DIL, DILSL, dil_qk(p + 1))
                pair_pe(pe, "dil", NDP - 1, U_DIL + 3 * (NDP - 1), DILSL, [])
                pe.wait_ge(sem("dil_mixed"), 4 * NDP + 1)
            else:
                pe.wait_ge(sem("mem_mixed"), 8 * NMP + 1)
                sgu_pe(pe)
                pe.wait_ge(*gup("xt_low", NT))

            for c in range(KT // 2):
                def ready(t):
                    if L == 0 and t == 0:
                        pe.wait_ge(sem("mix_low"), max(MIX_ORDER.index(2 * c), MIX_ORDER.index(2 * c + 1)) + 1)
                    if L == 1 and c == 0:
                        pe.wait_ge(*gup("mo_low", t + 1))
                u = U_OUT[L] + 2 * c
                acc_pe(pe, go[L], c, u,
                       lambda k, t: (XTh[:, 2 * c + k, t * P:(t + 1) * P], XTl[:, 2 * c + k, t * P:(t + 1) * P]),
                       [slot_of(u), slot_of(u + 1)], ready, after=norm_pe_after(pe, go[L]) if c == 3 else None)
            ffn_pe(pe, L, 0, True, False)
            with pe.Fori(1, NCH - 1) as c:
                ffn_pe(pe, L, c, False, False)
            ffn_pe(pe, L, NCH - 1, False, True)

    @block.scalar
    def _(act):
        for i in range(4):
            act.dma_start(XR[:, 2 * i:2 * i + 2, :], a["x"][0, 256 * i:256 * i + 256, :].rearrange("(t p) d -> p t d", p=P)
                          ).then_inc(sem(f"x_landed{i}"), 16)
            if i == 0:
                act.dma_start(ident[:, :], a["c_ident"]).then_inc(sem("const_landed"), 16)
        mem = a["mem"][0].rearrange("(t p) d -> p t d", p=P)
        act.dma_start(memraw[:, :, :], mem).then_inc(sem("mem_landed0"), 16)
        for t in range(NT):
            turn_act(act, gi, t)
        for t in range(2):
            turn_act(act, gm[0], t, high=memTh)
        for L in range(2):
            def mem_qk(p):
                return fills(lambda j: qk_act(act, "mem", NMP * L + p, j), "mem")

            def dil_qk(p):
                return fills(lambda j: qk_act(act, "dil", p, j), "dil")

            if L == 0:
                for f in mem_qk(0):
                    f()
            for p in range(NMP):
                pair_act(act, "mem", NMP * L + p, mem_qk(p + 1) if p < NMP - 1 else dil_qk(0) if L == 0 else [])
            if L == 0:
                with act.Fori(0, NDP - 1) as p:
                    pair_act(act, "dil", p, dil_qk(p + 1))

                def mix_high(i):
                    if i == 0:
                        act.wait_ge(sem("dil_v_proj"), 2 * NDP)
                        act.wait_ge(sem("dil_mixed"), 4 * (NDP - 1) + 1)
                    if i == KT - 1:
                        act.wait_ge(sem("dil_mixed"), 4 * NDP + 1)
                    j = MIX_ORDER[i]
                    src = mixT[:, j, :] if j < NDP else MO[:, j - NDP, :]
                    nc.scalar.activation(XTh[:, j, :], src, ACT.Copy).then_inc(sem("mix_high"), 1)

                pair_act(act, "dil", NDP - 1, [], lambda i: mix_high(i - 2) if 0 <= i - 2 < KT - 1 else None)
                mix_high(KT - 1)
                load_gb(act, go[0], a["ln_mix_g"][0], a["ln_mix_b"][0], gb)
            else:
                sgu_act(act)
            norm_act(act, go[L], False, ffn_beside(lambda i: ffn_silu(act, L, 0, i), lambda i: ffn_high(act, L, 0, i), L))
            act.wait_ge(*go[L]("shifted", NT))
            load_gb(act, gf[L], a["ln_ffn_g"][L], a["ln_ffn_b"][L], gb)
            if L == 0:
                act.wait_ge(sem("mix_low"), KT)
                act.dma_start(memraw[:, :, :], mem).then_inc(sem("mem_landed1"), 16)
            with act.Fori(1, NCH) as c:
                for i in range(4):
                    ffn_silu(act, L, c, i)
                    ffn_high(act, L, c, i)

            def beside(q):
                k_, q0, q1 = fills(lambda j: qk_act(act, "mem", NMP, j), "mem")
                if q == 3:
                    for t in range(2):
                        turn_act(act, gm[1], t, high=memTh)
                elif q == 5:
                    k_()
                elif q == 7:
                    act.wait_ge(*gf[0]("shifted", NT))
                    q0()
                    q1()

            norm_act(act, gf[L], L == 1, beside)

    @block.vector
    def _(dve):
        def attention_start(g, bf, times=1):
            for q in (bf.Qh, bf.Ql):
                nc.vector.memset(q[HD:P, 0, :].bitcast(F32), 0.0).then_inc(g("cleared"), 1)
                nc.vector.memset(q[0:HD, 1, :].bitcast(F32), 0.0).then_inc(g("cleared"), 1)
            for v in (bf.Vh, bf.Vl):
                nc.vector.memset(v[:, :, HD:2 * HD].bitcast(F32), 0.0).then_inc(g("cleared"), 1)
            dve.wait_ge(*g("cleared", 6 * times))
            if times == 1:
                dve.sem_inc(g("mixed"), 1)

        nc.vector.memset(eps[:, :], EPS).then_inc(sem("eps_set"), 1)
        for t in range(NT):
            turn_dve(dve, gi, t)
        def memory_start(L):
            g = pair_names("mem")
            nc.vector.memset(MemBuf.zero[:, :], 0.0).then_inc(g("zeroed"), 1)
            dve.wait_ge(*g("zeroed", L + 1))
            attention_start(g, MemBuf, L + 1)

        for t in range(2):
            turn_dve(dve, gm[0], t, high=memTh, low=memTl)
        dve.wait_ge(*gm[0]("xt_low", 2))
        memory_start(0)
        for L in range(2):
            def mem_qk(p):
                return fills(lambda j: qk_dve(dve, "mem", NMP * L + p, j), "mem")

            def dil_qk(p):
                return fills(lambda j: qk_dve(dve, "dil", p, j), "dil")

            if L == 0:
                attention_start(pair_names("dil"), DilBuf)
                for f in mem_qk(0):
                    f()
            for p in range(NMP):
                pair_dve(dve, "mem", NMP * L + p, mem_dst, mem_qk(p + 1) if p < NMP - 1 else dil_qk(0) if L == 0 else [])
            if L == 0:
                with dve.Fori(0, NDP - 1) as p:
                    pair_dve(dve, "dil", p, dil_dst, dil_qk(p + 1))

                def mix_low(i):
                    j = MIX_ORDER[i]
                    src = mixT[:, j, :] if j < NDP else MO[:, j - NDP, :]
                    dve.wait_ge(sem("mix_high"), i + 1)
                    nc.vector.tensor_tensor(XTl[:, j, :], src, XTh[:, j, :].bitcast(F32),
                                            ALU.subtract).then_inc(sem("mix_low"), 1)

                pair_dve(dve, "dil", NDP - 1, dil_dst, [], lambda i: mix_low(i - 2) if 0 <= i - 2 < KT - 1 else None)
                mix_low(KT - 1)
            else:
                sgu_dve(dve)
            for c in range(KT // 2 - 1):
                for t in range(NT):
                    if L == 0 and c == 0 and t % 2 == 0:
                        dve.wait_ge(sem(f"x_again{t // 2}"), 16)
                    acc_dve(dve, go[L], c, t, ALPHA if c == 0 else None)
            if L == 0:
                dve.sem_inc(gf[L]("gated"), 2)
                dve.sem_inc(gf[L]("hid_low"), 2)
                dve.sem_inc(gf[L]("added"), 4)
            norm_dve(dve, go[L], KT // 2 - 1, False,
                     ffn_beside(lambda i: ffn_gated(dve, L, 0, i), lambda i: ffn_low(dve, L, 0, i), L))
            for t in range(NT):
                acc_dve(dve, gf[L], 0, t, ALPHA)
            with dve.Fori(1, NCH - 1) as c:
                for i in range(4):
                    ffn_gated(dve, L, c, i)
                    ffn_low(dve, L, c, i)
                for t in range(NT):
                    acc_dve(dve, gf[L], c, t)
            for i in range(4):
                ffn_gated(dve, L, NCH - 1, i)
                ffn_low(dve, L, NCH - 1, i)

            def beside(q):
                k_, q0, q1 = fills(lambda j: qk_dve(dve, "mem", NMP, j), "mem")
                if q == 3:
                    for t in range(2):
                        turn_dve(dve, gm[1], t, high=memTh, low=memTl)
                elif q == 5:
                    k_()
                elif q == 7:
                    dve.wait_ge(*gf[0]("shifted", NT))
                    memory_start(1)
                    q0()
                    q1()

            norm_dve(dve, gf[L], NCH - 1, L == 1, beside)

    block.__exit__(None, None, None)


_INS = ["x", "mem", "a_w_in", "b_w_in", "sgu_ln_g", "sgu_ln_b", "sgu_w_s", "sgu_b_s", "w_mem_kv", "w_out",
        "ln_mix_g", "ln_mix_b", "w_gate", "w_up", "w_down", "ln_ffn_g", "ln_ffn_b"]


def kernel(**inputs):
    import concourse.bacc as bacc
    from concourse.bass_utils import run_bass_kernel_spmd

    nc = bacc.Bacc("TRN2", target_bir_lowering=False, num_devices=1)
    arrays = {n: np.ascontiguousarray(inputs[n]) for n in _INS}
    arrays.update(zip(("c_bias", "c_ident"), tables()))
    a = {n: nc.dram_tensor(f"in_{n}", v.shape, mybir.dt.from_np(v.dtype), kind="ExternalInput").ap()
         for n, v in arrays.items()}
    out = nc.dram_tensor("out_0", (1, S, D), F32, kind="ExternalOutput").ap()
    build(nc, a, out)
    r = run_bass_kernel_spmd(nc, [{f"in_{n}": v for n, v in arrays.items()}], core_ids=[0])
    return r.results[0]["out_0"]
```

```python
import numpy as np
import concourse.bass as bass
import concourse.mybir as mybir

F32 = mybir.dt.float32
F32R = mybir.dt.float32r
ALU = mybir.AluOpType
ACT = mybir.ActivationFunctionType

P = 128
S = 1024
D = 1024
M = 256
HD = 64
NT = S // P
KT = D // P
DIL_W = 768
MEM_W = 256
NDP = DIL_W // P
NMP = MEM_W // P
FF = 2816
NG = DIL_W // HD
NCH = FF // (2 * P)
ALPHA = float((2 * 2) ** 0.25)
EPS = 1e-5
PATTERNS = ((128, 1), (512, 4), (2048, 16))
UNIT = 1024
WS = 6
RS = 2
QSCALE = HD ** -0.5

U_MEM = (0, 98)
U_DIL = 6
U_V, U_U = 104, 110
U_OUT = (24, 116)
U_FFN = (32, 124)

KB = 1024
A_XTH, A_XTL, A_XR = 0, 32 * KB, 64 * KB
A_WH, A_WL, A_RAW = 96 * KB, 120 * KB, 144 * KB
A_MV, A_MO, A_X = 152 * KB, 176 * KB, 184 * KB
A_SMALL = 206 * KB


def tables():
    d = (np.arange(P)[:, None] - np.arange(S)[None, :] + (S - P)).astype(np.int64)
    count = np.zeros(d.shape, np.int64)
    for window, dil in PATTERNS:
        count += (d >= 0) & (d <= window) & (d % dil == 0)
    slopes = np.exp2(-8.0 * (np.arange(NG) + 1.0) / NG).astype(np.float32)
    bias = np.where(count > 0, np.log(np.maximum(count, 1)) - slopes[:, None, None].astype(np.float64) * d, -1e30)
    return bias.astype(np.float32), np.eye(P, dtype=np.float32)


def build(nc, a, out):
    base = -(-nc.sbuf_base // 64) * 64

    def at(name, shape, dt, off):
        return nc.alloc_sbuf_tensor_at(name, shape, dt, offset=base + off)

    sems = {}

    def sem(name):
        if name not in sems:
            sems[name] = nc.alloc_semaphore(name)
        return sems[name]

    XTh = at("XTh", [P, KT, S], F32R, A_XTH)
    XTl = at("XTl", [P, KT, S], F32R, A_XTL)
    XR = at("XR", [P, NT, D], F32, A_XR)
    Wh = at("Wh", [P, WS, UNIT], F32R, A_WH)
    Wl = at("Wl", [P, WS, UNIT], F32R, A_WL)
    raw = at("raw", [P, RS, UNIT], F32, A_RAW)
    PTh = at("PTh", [P, 2, 4, 2, P], F32R, A_WH + 12 * KB)
    Kh = at("Kh", [P, S], F32R, A_WH + 20 * KB)
    PTl = at("PTl", [P, 2, 4, 2, P], F32R, A_WL + 12 * KB)
    Kl = at("Kl", [P, S], F32R, A_WL + 20 * KB)
    mixT = at("mixT", [P, NDP, S], F32, A_MV)
    MO = at("MO", [P, NMP, S], F32, A_MO)
    memTh = at("memTh", [P, KT, M], F32R, A_MV)
    memTl = at("memTl", [P, KT, M], F32R, A_MV + 8 * KB)
    memraw = at("memraw", [P, 2, D], F32, A_MV + 16 * KB)

    class MemBuf:
        Qh = at("mQh", [P, 2, S], F32R, A_X)
        Ql = at("mQl", [P, 2, S], F32R, A_X + 8 * KB)
        Vh = at("mVh", [P, 2, 192], F32R, A_MV + 16 * KB)
        Vl = at("mVl", [P, 2, 192], F32R, A_MV + 16 * KB + 1536)
        Pb = at("mP", [P, 3, M], F32, A_MV + 19 * KB)
        vT = at("mvT", [P, M], F32, A_MV + 22 * KB)
        RB = at("mRB", [P, 2, 2, HD], F32, A_WH + 21 * KB)
        RSb = at("mRS", [P, 2 * P], F32, A_X + 16 * KB)
        zero = at("mzero", [P, M], F32, A_WH + 22 * KB)

    class DilBuf:
        Qh = at("dQh", [P, 2, S], F32R, A_XR)
        Ql = at("dQl", [P, 2, S], F32R, A_XR + 8 * KB)
        Vh = at("dVh", [P, NT, 192], F32R, A_XR + 16 * KB)
        Vl = at("dVl", [P, NT, 192], F32R, A_XR + 22 * KB)
        RB = at("dRB", [P, 2, 2, HD], F32, A_XR + 28 * KB)
        RSb = at("dRS", [P, 2 * P], F32, A_XR + 29 * KB)
        Pb = at("dP", [P, 3, S], F32, A_X)
        B = at("dB", [P, 2, S], F32, A_X + 12 * KB)
        vT = at("dvT", [P, S], F32, A_X + 8 * KB)

    gb = at("gb", [P, 2, D], F32, A_X)
    g_mem = at("g_mem", [P, 1, D], F32, A_MO + 4 * KB)
    b_mem = at("b_mem", [P, 1, D], F32, A_X + 18 * KB)
    fbuf = at("fbuf", [P, 3, 512], F32, A_X + 8 * KB)
    hidh = at("hidh", [P, 2, S], F32R, A_MV)
    hidl = at("hidl", [P, 2, S], F32R, A_MV + 8 * KB)
    silu = at("silu", [P, 2, 512], F32, A_MO)
    hid = at("hid", [P, 2, 512], F32, A_MO + 4 * KB)
    V = at("V", [P, NT, DIL_W], F32, A_MV)
    WSh = at("WSh", [P, NG, P], F32R, A_X)
    WSl = at("WSl", [P, NG, P], F32R, A_X + 6 * KB)
    wsraw = at("wsraw", [P, NG, P], F32, A_X + 12 * KB)
    sgb = at("sgb", [P, 2, DIL_W], F32, A_X + 12 * KB)
    VSh = at("VSh", [P, 2, NT, HD], F32R, A_X + 12 * KB)
    VSl = at("VSl", [P, 2, NT, HD], F32R, A_X + 16 * KB)
    ub = at("ub", [P, 2, M], F32, A_X + 20 * KB)
    small_at = [A_SMALL]

    def small(name, shape):
        n = 4 * int(np.prod(shape[1:]))
        t = at(name, shape, F32, small_at[0])
        small_at[0] += -(-n // 32) * 32
        return t

    ident = small("ident", [P, P])
    mneg = small("mneg", [P, 16])
    den = small("den", [P, 16])
    rden = small("rden", [P, 16])
    st = small("st", [P, NT, 3, 6])
    mv = small("mv", [P, NT, 2])
    rstd = small("rstd", [P, NT])
    nmr = small("nmr", [P, NT])
    bst = small("bst", [P, NG])
    gcol = small("gcol", [P, 2, KT])
    eps = small("eps", [P, 1])
    zcol = small("zcol", [P, 1])
    tick = small("tick", [P, 16])
    ps = nc.alloc_psum_tensor("ps", [P, 8 * 512], F32)

    def bank(b, n=512, off=0):
        return ps[:, 512 * b + off:512 * b + off + n]

    def cols(w, c0):
        return w[:, bass.ds(c0, P)].rearrange("(k p) c -> p k c", p=P)

    def load(sp, u, src):
        if not (isinstance(u, int) and u < RS):
            sp.wait_ge(split_done, u - RS + 1)
        slot = load.turn % RS
        load.turn += 1
        dst = raw[:, slot, :]
        if len(src.shape) == 3:
            dst = dst.rearrange("p (k c) -> p k c", c=P)
        sp.dma_start(dst, src).then_inc(raw_landed[slot], 16)

    load.turn = 0
    split_done = sem("split_done")
    raw_landed = [sem(f"raw_landed{i}") for i in range(RS)]

    def used(u, c=None):
        for L in range(2):
            v = u - U_MEM[L]
            if 0 <= v < 3 * NMP:
                p = v // 3 + NMP * L
                return (sem("mem_v_proj"), p + 1) if v % 3 == 2 else (sem("mem_qk_proj"), 3 * p + (3, 2)[v % 3])
            v = u - U_OUT[L]
            if 0 <= v < KT:
                return go[L]("product", 16 * (v // 2 + 1))
            v = u - U_FFN[L]
            if 0 <= v < 6 * NCH:
                c, j = (v // 6, v % 6) if c is None else (c, v)
                if j < 4:
                    return gf[L]("up", 4 * c + 3 + j // 2)
                return gf[L]("product", 16 * (c + 1))
        v = u - U_DIL
        if 0 <= v < 3 * NDP:
            p = v // 3
            return (sem("dil_v_proj"), 2 * p + 2) if v % 3 == 2 else (sem("dil_qk_proj"), 4 * p + 2 + 2 * (v % 3))
        if u < U_U:
            return sem("vproj_product"), NT * ((u - U_V) // 2 + 1)
        return sem("uproj_product"), NT * ((u - U_U) // 2 + 1)

    def slot_of(u):
        if u < U_OUT[0]:
            return u % 3
        if u < U_MEM[1]:
            return u % WS
        return [2, 3, 4, 0, 1, 2][u - U_MEM[1]] if u < U_V else (u - U_V) % WS

    def user_before(u):
        return max((v for v in range(u) if slot_of(v) == slot_of(u)), default=None)

    def split(pool, u, before=None, turn=None, rounds=None, slot=None):
        if slot is None:
            slot = slot_of(u)
            before = user_before(u) if before is None else before
        turn = u % RS if turn is None else turn
        pool.wait_ge(raw_landed[turn], 16 * (u // RS + 1) if rounds is None else 16 * rounds)
        if before is not None:
            pool.wait_ge(*(before if isinstance(before, tuple) else used(before)))
        nc.gpsimd.tensor_tensor(Wh[:, slot, :], raw[:, turn, :], zcol[:, 0:1].to_broadcast([P, UNIT]),
                                ALU.add).then_inc(high_done, 1)
        pool.wait_ge(high_done, u + 1)
        nc.gpsimd.tensor_tensor(Wl[:, slot, :], raw[:, turn, :], Wh[:, slot, :].bitcast(F32),
                                ALU.subtract).then_inc(split_done, 1)

    high_done = sem("high_done")

    def three(dst, wh, wl, xh, xl, first, last):
        nc.tensor.matmul(dst, wh, xh, start=first, stop=False)
        nc.tensor.matmul(dst, wh, xl, start=False, stop=False)
        return nc.tensor.matmul(dst, wl, xh, start=False, stop=last)

    def wtile(slot, k):
        return Wh[:, slot, k * P:(k + 1) * P], Wl[:, slot, k * P:(k + 1) * P]

    def rows_in(dst, slot, xh, xl, lo, n):
        for k in range(KT):
            wh, wl = wtile(slot, k)
            mm = three(dst, wh, wl, xh[:, k, lo:lo + n], xl[:, k, lo:lo + n], k == 0, k == KT - 1)
        return mm

    def tile_of(n):
        return 2 * (n // 4) + n % 2, (n // 2) % 2

    def width(kind, n):
        return M if kind == "mem" else P * (tile_of(n)[0] + 1)

    def keytiles(kind, s):
        return 2 if kind == "mem" else 2 * (s // 2) + 2

    def items(kind):
        found = []
        for s in range(8):
            nk = keytiles(kind, s)
            for lo in range(0, nk, 4):
                found.append((s, lo, min(4, nk - lo), lo == 0, lo + 4 >= nk))
        return found

    def item_of(kind, s):
        return max(i for i, it in enumerate(items(kind)) if it[0] == s)

    def blocks(kind, it, i):
        s, lo, nk, _, last = it
        return nk - 1 if kind == "dil" and last and i == 0 else nk

    def pair_names(kind):
        def g(name, value=None):
            s = sem(f"{kind}_{name}")
            return s if value is None else (s, value)
        return g

    def qk_groups(kind):
        if kind == "mem":
            return [("q", 0, 0), ("k", 0, 2), ("q", 1, 1)]
        return [("q", 0, 0), ("q", 1, 1), ("k", 0, 2), ("k", 1, 3)]

    def s_banks(kind, n):
        if kind == "mem" or n < 8:
            return [n % 4], max(0, n - 3)
        return [2 * (n % 2), 2 * (n % 2) + 1], {8: 6, 9: 8}.get(n, n - 1)

    def s_view(kind, n):
        w, b = width(kind, n), s_banks(kind, n)[0][0]
        if w > 512:
            return ps[:, 512 * b:512 * b + 1024].rearrange("p (a c) -> p a c", c=512)[:, :, 0:w // 2]
        return bank(b, w)

    def qk_pe(pe, kind, j, u, slots):
        what, h, b = qk_groups(kind)[j]
        un = "qk".index(what)
        pe.wait_ge(split_done, u + un + 1)
        if what == "k" and kind == "mem":
            mm = rows_in(bank(b, M), slots[un], memTh, memTl, 0, M)
        else:
            mm = rows_in(bank(b), slots[un], XTh, XTl, h * 512, 512)
        mm.then_inc(sem(f"{kind}_qk_proj"), 1)

    def qk_act(act, kind, pi, j):
        g = pair_names(kind)
        bf = MemBuf if kind == "mem" else DilBuf
        what, h, b = qk_groups(kind)[j]
        act.wait_ge(*g("qk_proj", pi * len(qk_groups(kind)) + j + 1))
        if what == "q":
            for hd in range(2):
                r = slice(HD * hd, HD * hd + HD)
                nc.scalar.activation(bf.Qh[r, hd, h * 512:h * 512 + 512], bank(b)[r, :], ACT.Copy,
                                     scale=QSCALE).then_inc(g("q_high"), 1)
        else:
            n = M if kind == "mem" else 512
            nc.scalar.activation(Kh[:, h * 512:h * 512 + n], bank(b, n), ACT.Copy).then_inc(g("k_high"), 1)

    def qk_dve(dve, kind, pi, j):
        g = pair_names(kind)
        bf = MemBuf if kind == "mem" else DilBuf
        what, h, b = qk_groups(kind)[j]
        if what == "q":
            for hd in range(2):
                dve.wait_ge(*g("q_high", pi * 4 + 2 * h + hd + 1))
                r = slice(HD * hd, HD * hd + HD)
                cs = slice(h * 512, h * 512 + 512)
                nc.vector.scalar_tensor_tensor(bf.Ql[r, hd, cs], bank(b)[r, :], QSCALE,
                                               bf.Qh[r, hd, cs].bitcast(F32), ALU.mult,
                                               ALU.subtract).then_inc(g("q_low"), 1)
        else:
            n, nh = (M, 1) if kind == "mem" else (512, 2)
            dve.wait_ge(*g("k_high", pi * nh + h + 1))
            cs = slice(h * 512, h * 512 + n)
            nc.vector.tensor_tensor(Kl[:, cs], bank(b, n), Kh[:, cs].bitcast(F32), ALU.subtract).then_inc(g("k_low"), 1)

    def pair_pe(pe, kind, pi, u, slots, fill):
        g = pair_names(kind)
        bf = MemBuf if kind == "mem" else DilBuf
        Kn = M if kind == "mem" else S
        nh = 1 if kind == "mem" else 2
        its = items(kind)
        NI = len(its)

        def scores(n):
            qt, hd = tile_of(n)
            w = width(kind, n)
            banks, free = s_banks(kind, n)
            if free:
                pe.wait_ge(*g("logits", pi * 16 + free))
            nb = max(256, w) if w <= 512 else w // 2
            for i in range(1 if w <= 512 else 2):
                dst = bank(banks[i], nb)
                ks = slice(i * nb, (i + 1) * nb)
                q0 = slice(qt * P, (qt + 1) * P)
                mm = three(dst, bf.Qh[:, hd, q0], bf.Ql[:, hd, q0], Kh[:, ks], Kl[:, ks], True, True)
            mm.then_inc(g("scores"), 1)

        def turn(i, ab):
            s, lo, nk, first, last = its[i]
            if first:
                pe.wait_ge(*g("probs", pi * 16 + 2 * s + ab + 1))
            if i >= 1:
                pe.wait_ge(*g("pt_low", pi * 2 * NI + 2 * (i - 1) + ab + 1))
            for k in range(blocks(kind, its[i], ab)):
                mm = nc.tensor.transpose(bank(4 + ab, P, k * P),
                                         bf.Pb[:, (2 * s + ab) % 3, (lo + k) * P:(lo + k + 1) * P], ident[:, :])
            mm.then_inc(g("turned"), 1)

        def pv(i):
            s, lo, nk, first, last = its[i]
            c, hd = s // 2, s % 2
            pe.wait_ge(*g("pt_low", pi * 2 * NI + 2 * i + 2))
            if i == 0:
                pe.wait_ge(*g("v_low", (pi + 1) * nh))
            if kind == "dil" and last:
                pe.wait_ge(*g("pt_zero", (pi * 8 + s + 1) * 2))
            if hd == 0 and first and c >= 2:
                pe.wait_ge(*g("mixed", pi * 4 + c))
            dst = bank(6 + c % 2, 2 * P)
            for k in range(nk):
                mm = three(dst, bf.Vh[:, lo + k, HD * hd:HD * hd + P], bf.Vl[:, lo + k, HD * hd:HD * hd + P],
                           PTh[:, i % 2, k, :, :], PTl[:, i % 2, k, :, :],
                           hd == 0 and first and k == 0, hd == 1 and last and k == nk - 1)
            mm.then_inc(g("pv"), 1)
            if hd == 1 and last:
                pe.wait_ge(*g("rden_wide", pi * 4 + c + 1))
                for q in range(2):
                    mm = nc.tensor.transpose(bank(6 + c % 2, P, 256 + q * P),
                                             bf.RB[:, q, :, :].rearrange("p a d -> p (a d)"), ident[:, :])
                mm.then_inc(g("rden_turned"), 1)

        def values(h):
            if h == 0:
                pe.wait_ge(split_done, u + 3)
            if kind == "mem":
                mm = rows_in(bank(4, M), slots[2], memTh, memTl, 0, M)
            else:
                mm = rows_in(bank(4 + h), slots[2], XTh, XTl, h * 512, 512)
            mm.then_inc(g("v_proj"), 1)

        pe.wait_ge(*g("mixed", pi * 4 + 1))
        values(0)
        pe.wait_ge(*g("k_low", (pi + 1) * nh))
        pe.wait_ge(*g("q_low", (pi + 1) * 4))
        scores(0)
        if nh == 2:
            values(1)
        scores(1)
        for t in range(Kn // P):
            if t % 4 == 0:
                pe.wait_ge(*g("v_copied", pi * nh + t // 4 + 1))
            mm = nc.tensor.transpose(bank(6 + t // 4, P, (t % 4) * P), bf.vT[:, t * P:(t + 1) * P], ident[:, :])
            if t % 4 == 3 or t == Kn // P - 1:
                mm.then_inc(g("v_turned"), 1)
        for i, (s, lo, nk, first, last) in enumerate(its):
            if first and s < 7:
                scores(2 * s + 2)
                if last:
                    scores(2 * s + 3)
            if first:
                turn(i, 0)
            turn(i, 1)
            if first and not last:
                if s < 7:
                    scores(2 * s + 3)
                turn(i + 1, 0)
            if i >= 1:
                pv(i - 1)
        if fill:
            fill[0]()
        pv(NI - 1)
        for f in fill[1:]:
            f()

    def pair_act(act, kind, pi, fill):
        g = pair_names(kind)
        bf = MemBuf if kind == "mem" else DilBuf
        Kn = M if kind == "mem" else S
        nh = 1 if kind == "mem" else 2
        its = items(kind)
        NI = len(its)

        def v_copy(h):
            act.wait_ge(*g("v_proj", pi * nh + h + 1))
            n = min(512, Kn)
            nc.scalar.activation(bf.vT[:, h * 512:h * 512 + n], bank(4 + h, n), ACT.Copy).then_inc(g("v_copied"), 1)

        def v_high(j):
            act.wait_ge(*g("v_turned", pi * nh + j + 1))
            m = min(4, Kn // P)
            src = bank(6 + j, m * P).rearrange("p (t a d) -> p t a d", a=2, d=HD)
            for hd in range(2):
                nc.scalar.activation(bf.Vh[:, 4 * j:4 * j + m, 2 * HD * hd:2 * HD * hd + HD],
                                     src[:, :, hd, :], ACT.Copy).then_inc(g("v_high"), 1)

        def exp(n):
            act.wait_ge(*g("logits", pi * 16 + n + 1))
            p = bf.Pb[:, n % 3, 0:width(kind, n)]
            nc.scalar.activation(p, p, ACT.Exp, bias=mneg[:, n:n + 1], scale=-1.0,
                                 accum_out=den[:, n:n + 1]).then_inc(g("probs"), 1)

        def pt_high(i, ab):
            act.wait_ge(*g("turned", pi * 2 * NI + 2 * i + ab + 1))
            if i >= 2:
                act.wait_ge(*g("pv", pi * NI + i - 1))
            k = blocks(kind, its[i], ab)
            if k:
                nc.scalar.activation(PTh[:, i % 2, 0:k, ab, :], bank(4 + ab, k * P).rearrange("p (k q) -> p k q", q=P),
                                     ACT.Copy).then_inc(g("pt_high"), 1)

        def rden_copy(c):
            act.wait_ge(*g("rden_turned", pi * 4 + c + 1))
            nc.scalar.activation(bf.RSb[:, :], bank(6 + c % 2, 256, 256), ACT.Copy).then_inc(g("rden_copied"), 1)

        v_copy(0)
        exp(0)
        if nh == 2:
            v_copy(1)
        exp(1)
        for j in range(nh):
            v_high(j)
        for i, (s, lo, nk, first, last) in enumerate(its):
            pt_high(i, 0)
            if first and last and s < 7:
                exp(2 * s + 2)
            if last and not first and s < 7:
                exp(2 * s + 3)
            pt_high(i, 1)
            if first and not last and s < 7:
                exp(2 * s + 2)
            if first and last and s < 7:
                exp(2 * s + 3)
            if last and s % 2 == 0 and s >= 2:
                rden_copy(s // 2 - 1)
        if fill:
            fill[0]()
        rden_copy(3)
        for f in fill[1:]:
            f()

    def pair_dve(dve, kind, pi, dst, fill, beside=lambda i: None):
        g = pair_names(kind)
        bf = MemBuf if kind == "mem" else DilBuf
        nh = 1 if kind == "mem" else 2
        its = items(kind)
        NI = len(its)

        def v_low(j):
            dve.wait_ge(*g("v_high", (pi * nh + j + 1) * 2))
            m = 2 if kind == "mem" else 4
            src = bank(6 + j, m * P).rearrange("p (t a d) -> p t a d", a=2, d=HD)
            for hd in range(2):
                vs = (slice(None), slice(4 * j, 4 * j + m), slice(2 * HD * hd, 2 * HD * hd + HD))
                ins = nc.vector.tensor_tensor(bf.Vl[vs], src[:, :, hd, :], bf.Vh[vs].bitcast(F32), ALU.subtract)
            ins.then_inc(g("v_low"), 1)

        def logits(n):
            qt, hd = tile_of(n)
            w = width(kind, n)
            dve.wait_ge(*g("scores", pi * 16 + n + 1))
            if n == 2:
                dve.wait_ge(*g("v_turned", (pi + 1) * nh))
            if n >= 3:
                dve.wait_ge(*g("turned", pi * 2 * NI + 2 * item_of(kind, (n - 3) // 2) + (n - 3) % 2 + 1))
            if kind == "dil":
                if n == 0 or n == 2:
                    dve.wait_ge(*g(f"bias_landed{hd}", (pi + 1) * 16))
                bias = bf.B[:, hd, S - P - qt * P:S - P - qt * P + w]
            else:
                bias = bf.zero[:, :]
            nc.vector.memset(tick[:, n:n + 1], 0.0)
            o = bf.Pb[:, n % 3, 0:w]
            if w > 512:
                bias = bias.rearrange("p (a c) -> p a c", a=2)
                o = o.rearrange("p (a c) -> p a c", a=2)
            nc.vector.tensor_tensor_reduce(o, s_view(kind, n), bias, -1.0, 3e38, ALU.add, ALU.min,
                                           mneg[:, n:n + 1]).then_inc(g("logits"), 1)

        def pt_low(i, ab):
            dve.wait_ge(*g("pt_high", pi * 2 * NI + 2 * i + ab + 1))
            k = blocks(kind, its[i], ab)
            nc.vector.tensor_tensor(PTl[:, i % 2, 0:k, ab, :], bank(4 + ab, k * P).rearrange("p (k q) -> p k q", q=P),
                                    PTh[:, i % 2, 0:k, ab, :].bitcast(F32), ALU.subtract).then_inc(g("pt_low"), 1)

        def zero(i):
            if i >= 2:
                dve.wait_ge(*g("pv", pi * NI + i - 1))
            k = its[i][2] - 1
            nc.vector.memset(PTh[:, i % 2, k, 0, :].bitcast(F32), 0.0).then_inc(g("pt_zero"), 1)
            nc.vector.memset(PTl[:, i % 2, k, 0, :].bitcast(F32), 0.0).then_inc(g("pt_zero"), 1)

        def rden_of(c):
            t0 = 4 * c
            dve.wait_ge(*g("probs", pi * 16 + t0 + 4))
            if c >= 1:
                dve.wait_ge(*g("rden_turned", pi * 4 + c))
            nc.vector.reciprocal(rden[:, t0:t0 + 4], den[:, t0:t0 + 4]).then_inc(g("rden"), 1)
            dve.wait_ge(*g("rden", pi * 4 + c + 1))
            src = rden[:, t0:t0 + 4].rearrange("p (h i) -> p i h", h=2).unsqueeze(3).to_broadcast([P, 2, 2, HD])
            nc.vector.tensor_copy(bf.RB[:, :, :, :], src).then_inc(g("rden_wide"), 1)

        def mix(c):
            dve.wait_ge(*g("rden_copied", pi * 4 + c + 1))
            nc.vector.tensor_tensor(dst(pi, c), bank(6 + c % 2, 256), bf.RSb[:, :], ALU.mult).then_inc(g("mixed"), 1)

        logits(0)
        logits(1)
        for j in range(nh):
            v_low(j)
        for i, (s, lo, nk, first, last) in enumerate(its):
            if first and s < 7:
                logits(2 * s + 2)
            if last and not first and s < 7:
                logits(2 * s + 3)
            if last and kind == "dil":
                zero(i)
            pt_low(i, 0)
            if first and last and s < 7:
                logits(2 * s + 3)
            pt_low(i, 1)
            if last and s % 2 == 0 and s >= 2:
                mix(s // 2 - 1)
            if last and s % 2 == 1:
                rden_of(s // 2)
            beside(i)
        if fill:
            fill[0]()
        mix(3)
        for f in fill[1:]:
            f()

    def fills(make, kind):
        return [lambda j=j: make(j) for j in range(len(qk_groups(kind)))]

    def mem_dst(pi, c):
        return MO[:, pi % NMP, c * 256:(c + 1) * 256]

    def dil_dst(pi, c):
        return mixT[:, bass.ds(pi, 1), c * 256:(c + 1) * 256].rearrange("p a c -> p (a c)")

    def turn_pe(pe, g, t, src, nk=KT, bb=0):
        if t >= 2:
            pe.wait_ge(*g("xt_low", t - 1))
        b = bb + 2 * (t % 2)
        for k in range(nk):
            mm = nc.tensor.transpose(bank(b + k // 4, P, (k % 4) * P), src[:, k * P:(k + 1) * P], ident[:, :])
        mm.then_inc(g("xt_turned"), 1)

    def turned(t, nk, bb):
        b = bb + 2 * (t % 2)
        return ps[:, 512 * b:512 * b + nk * P].rearrange("p (k q) -> p k q", q=P)

    def turn_act(act, g, t, nk=KT, bb=0, high=XTh):
        act.wait_ge(*g("xt_turned", t + 1))
        nc.scalar.activation(high[:, 0:nk, t * P:(t + 1) * P], turned(t, nk, bb), ACT.Copy).then_inc(g("xt_high"), 1)

    def turn_dve(dve, g, t, nk=KT, bb=0, high=XTh, low=XTl):
        dve.wait_ge(*g("xt_high", t + 1))
        nc.vector.tensor_tensor(low[:, 0:nk, t * P:(t + 1) * P], turned(t, nk, bb),
                                high[:, 0:nk, t * P:(t + 1) * P].bitcast(F32), ALU.subtract).then_inc(g("xt_low"), 1)

    def acc_pe(pe, g, c, u, lhs, slots, ready, after=None, tiles=range(NT)):
        pe.wait_ge(split_done, u + 2)
        for t in tiles:
            ready(t)
            for h in range(2):
                n = 2 * t + h
                if not (isinstance(c, int) and c * 16 + n < 4):
                    pe.wait_ge(*g("added", c * 16 + n - 3 + g.credit))
                for k in range(2):
                    lh, ll = lhs(k, t)
                    mm = three(bank(4 + n % 4), lh, ll, Wh[:, slots[k], h * 512:(h + 1) * 512],
                               Wl[:, slots[k], h * 512:(h + 1) * 512], k == 0, k == 1)
                mm.then_inc(g("product"), 1)
            if after:
                after(t)

    def acc_dve(dve, g, c, t, scaled=None):
        for h in range(2):
            n = 2 * t + h
            dve.wait_ge(*g("product", c * 16 + n + 1))
            x = XR[:, t, h * 512:(h + 1) * 512]
            if scaled:
                nc.vector.scalar_tensor_tensor(x, x, scaled, bank(4 + n % 4), ALU.mult, ALU.add).then_inc(g("added"), 1)
            else:
                nc.vector.tensor_tensor(x, x, bank(4 + n % 4), ALU.add).then_inc(g("added"), 1)

    def row_bank(g, j):
        if j < KT and g is gf[0]:
            return 4 + j % 4, (j - 4 if j >= 4 else None)
        if j < KT:
            return (j, None) if j < 4 else (2 + j % 2, j - 2)
        return 4 + (j + 2) % 4, (j - 4 if j >= KT + 4 else None)

    def row_turn(pe, g, j, c):
        h, k = j // KT, j % KT
        if k == 0:
            pe.wait_ge(*g("normed", 4 * h + 4))
        if j == KT or (j == 0 and g is gf[0]):
            pe.wait_ge(*g("added", c * 16 + 8 * (h + 1 if g is gf[0] else 2) + g.credit))
        b, before = row_bank(g, j)
        if before is not None:
            pe.wait_ge(*g("affine", before + 1))
        for i in range(4):
            mm = nc.tensor.transpose(bank(b, P, i * P), XR[:, 4 * h + i, k * P:(k + 1) * P], ident[:, :])
        mm.then_inc(g("row_turned"), 1)

    def norm_pe_after(pe, g, c):
        def after(t):
            for j in {6: range(4), 7: (4, 5)}.get(t, ()):
                row_turn(pe, g, j, c)
        return after

    def xt_unit(x, j):
        return x[:, j % KT, 512 * (j // KT):512 * (j // KT) + 512]

    def row_act(act, g, j):
        act.wait_ge(*g("row_turned", j + 1))
        if j == 0:
            act.wait_ge(*g("col_landed", 32))
        if j >= 3:
            act.wait_ge(*g("xt_low", j - 2))
        k = j % KT
        nc.scalar.activation(fbuf[:, j % 3, :], bank(row_bank(g, j)[0]), ACT.Identity, bias=gcol[:, 1, k:k + 1],
                             scale=gcol[:, 0, k:k + 1]).then_inc(g("affine"), 1)

    def row_pool(pool, g, units):
        for j in units:
            pool.wait_ge(*g("affine", j + 1))
            nc.gpsimd.tensor_tensor(xt_unit(XTh, j), fbuf[:, j % 3, :], zcol[:, 0:1].to_broadcast([P, 512]),
                                    ALU.add).then_inc(g("xt_high"), 1)

    def row_dve(dve, g, j):
        dve.wait_ge(*g("xt_high", j + 1))
        nc.vector.tensor_tensor(xt_unit(XTl, j), fbuf[:, j % 3, :], xt_unit(XTh, j).bitcast(F32),
                                ALU.subtract).then_inc(g("xt_low"), 1)

    DVE_GAIN, DVE_SHIFT = (7,), (1, 3, 5, 6, 7)

    def shifted(g, t):
        if g is gf[1] and t in DVE_SHIFT:
            return sem("final_dve"), DVE_SHIFT.index(t) + 1
        n = t if g is not gf[1] else sum(q not in DVE_SHIFT for q in range(t))
        return g("shifted", n + 1)

    UNITS_AT = {5: (0, 1, 2, 3), 6: (4, 5, 6, 7)}

    def norm_dve(dve, g, c, tiles, units=()):
        nself = 3 * tiles[0]
        for t in list(tiles) + [tiles[-1] + 1]:
            if t in tiles:
                acc_dve(dve, g, c, t)
                dve.wait_ge(*g("added", c * 16 + 2 * t + 2 + g.credit))
                for h in range(2):
                    nc.vector.bn_stats(st[:, t, h, :], XR[:, t, h * 512:(h + 1) * 512]).then_inc(g("ln_self"), 1)
                nself += 2
                dve.wait_ge(*g("ln_self", nself))
                nc.vector.bn_aggr(mv[:, t, :], st[:, t, 0:2, :].rearrange("p a b -> p (a b)")).then_inc(g("stats"), 1)
            if t > tiles[0]:
                q = t - 1
                dve.wait_ge(*g("root", t))
                nc.vector.reciprocal(rstd[:, q:q + 1], rstd[:, q:q + 1]).then_inc(g("ln_self"), 1)
                nself += 1
                dve.wait_ge(*g("ln_self", nself))
                nc.vector.tensor_scalar(nmr[:, q:q + 1], mv[:, q, 0:1], rstd[:, q:q + 1], -1.0, ALU.mult,
                                        ALU.mult).then_inc(g("rstd"), 1)
            if t in units:
                for j in units[t]:
                    row_dve(dve, g, j)

    def final_dve(dve, q):
        g = gf[1]
        if q in DVE_GAIN:
            dve.wait_ge(*g("normed", q + 1))
            nc.vector.tensor_tensor(XR[:, q, :], XR[:, q, :], gb[:, 0, :], ALU.mult).then_inc(sem("final_gain"), 1)
            dve.wait_ge(sem("final_gain"), DVE_GAIN.index(q) + 1)
        elif q in DVE_SHIFT:
            dve.wait_ge(*g("gained", q + 1))
        if q in DVE_SHIFT:
            nc.vector.tensor_tensor(XR[:, q, :], XR[:, q, :], gb[:, 1, :], ALU.add).then_inc(sem("final_dve"), 1)

    def norm_act(act, g, tiles, units=()):
        for t in list(tiles) + [tiles[-1] + 1]:
            if t in tiles:
                act.wait_ge(*g("stats", t + 1))
                nc.scalar.activation(rstd[:, t:t + 1], mv[:, t, 1:2], ACT.Sqrt, bias=eps[:, 0:1]).then_inc(g("root"), 1)
            if t > tiles[0]:
                q = t - 1
                act.wait_ge(*g("rstd", t))
                nc.scalar.activation(XR[:, q, :], XR[:, q, :], ACT.Identity, bias=nmr[:, q:q + 1],
                                     scale=rstd[:, q:q + 1]).then_inc(g("normed"), 1)
            if t in units:
                for j in units[t]:
                    row_act(act, g, j)

    def norm_pool(pool, g, tiles, done=0, last=False):
        pool.wait_ge(*g("gb_landed", 32))
        gain, shift = (g_mem[:, 0, :], b_mem[:, 0, :]) if g is gf[0] else (gb[:, 0, :], gb[:, 1, :])
        for n, t in enumerate(tiles, done):
            if last:
                pool.wait_ge(*g("normed", t + 1))
                if t in DVE_GAIN:
                    continue
            else:
                pool.wait_ge(*g("row_turned", KT * (t // 4 + 1)))
            nc.gpsimd.tensor_tensor(XR[:, t, :], XR[:, t, :], gain, ALU.mult).then_inc(g("gained"), 1)
            if last and t in DVE_SHIFT:
                continue
            pool.wait_ge(*g("gained", n + 1))
            nc.gpsimd.tensor_tensor(XR[:, t, :], XR[:, t, :], shift, ALU.add).then_inc(g("shifted"), 1)

    def odd_rows_dve(dve, g, t):
        dve.wait_ge(*g("gb_landed", 32))
        dve.wait_ge(*g("row_turned", KT * (t // 4 + 1)))
        nc.vector.tensor_tensor(XR[:, t, :], XR[:, t, :], gb[:, 0, :], ALU.mult).then_inc(g("odd_gained"), 1)
        dve.wait_ge(*g("odd_gained", t // 2 + 1))
        nc.vector.tensor_tensor(XR[:, t, :], XR[:, t, :], gb[:, 1, :], ALU.add).then_inc(g("odd_shifted"), 1)

    def load_cols(eng, g, gain, shift):
        with nc.allow_non_contiguous_dma(reason="1024 gains and shifts, once"):
            for i, w in enumerate((gain, shift)):
                eng.dma_start(gcol[:, i, :], w.rearrange("(k p) -> p k", p=P)).then_inc(g("col_landed"), 16)

    def load_row(eng, g, w, dst):
        n = w.shape[0]
        eng.dma_start(dst, w.rearrange("(a n) -> a n", a=1).to_broadcast([P, n])).then_inc(g("gb_landed"), 16)

    def load_gb(eng, g, gain, shift, dst):
        load_row(eng, g, gain, dst[:, 0, :])
        load_row(eng, g, shift, dst[:, 1, :])

    class Names:
        def __init__(self, phase, rises=(), layer=0, credit=0):
            self.phase, self.rises, self.layer, self.credit = phase, dict(rises), layer, credit

        def __call__(self, name, value=None):
            s = sem(f"{self.phase}_{name}")
            return s if value is None else (s, value + self.layer * self.rises.get(name, 0))

    NORM = {"row_turned": 2 * KT, "affine": 2 * KT, "xt_high": 2 * KT, "xt_low": 2 * KT, "stats": NT, "root": NT,
            "rstd": NT, "normed": NT, "gained": NT, "shifted": NT, "ln_self": 3 * NT, "gb_landed": 32,
            "col_landed": 32}
    OUT = {**NORM, **{x: NT // 2 for x in ("gained", "shifted", "odd_gained", "odd_shifted")}, "product": 16 * KT // 2, "added": 16 * KT // 2}
    FFN = {**NORM, "product": 16 * NCH, "added": 16 * NCH,
           **{x: 4 * NCH for x in ("gate", "up", "silu", "gated", "hid_high", "hid_low")}}
    gi = Names("in")
    gm = [Names("memory", {"xt_turned": 2, "xt_high": 2, "xt_low": 2}, L) for L in range(2)]
    go = [Names("out", OUT, L) for L in range(2)]
    gf = [Names("ffn", FFN, L, 4) for L in range(2)]

    def ffn_slots(L):
        return [slot_of(U_FFN[L] + j) for j in range(6)]

    def ffn_pe(pe, L, c, first, last):
        g = gf[L]
        sl = ffn_slots(L)
        u = U_FFN[L] + c * 6
        start = 0

        def ready(t):
            if t % 4 == 0:
                pe.wait_ge(*g("hid_low", c * 4 + 2 * (t // 4) + 2 + 2))

        def products(tiles):
            acc_pe(pe, g, c, u + 4, lambda k, t: (hidh[:, k, t * P:(t + 1) * P], hidl[:, k, t * P:(t + 1) * P]),
                   sl[4:6], ready, tiles=tiles)

        if first:
            pe.wait_ge(split_done, u + 2)
            for k in range(KT):
                if k in (3, 4):
                    row_turn(pe, go[L], 3 + k, None)
                pe.wait_ge(*go[L]("xt_low", k + 1))
                for j, name in enumerate(("gate", "up")):
                    mm = three(bank(j), *wtile(sl[j], k), XTh[:, k, 0:512], XTl[:, k, 0:512], k == 0, k == KT - 1)
                    if k == KT - 1:
                        mm.then_inc(g(name), 1)
            start = 1
        for i in range(start, 4):
            h, m = i // 2, i % 2
            if first and i == 2:
                pe.wait_ge(*go[L]("xt_low", 2 * KT))
            if h == 0:
                pe.wait_ge(split_done, u + 2 * m + 2)
            pe.wait_ge(*g("gated", c * 4 + i - 2 + 1 + 2))
            for j, name in enumerate(("gate", "up")):
                for k in range(KT):
                    if first and i == 1 and k == (5, 2)[j]:
                        for q in range(4):
                            row_turn(pe, go[L], KT + 4 * j + q, KT // 2 - 1)
                    if last and L == 0 and (i, j, k) in ((3, 0, 0), (3, 0, 5)):
                        for q in range(4):
                            row_turn(pe, g, 4 * (k > 0) + q, c)
                    mm = three(bank(2 * (i % 2) + j), *wtile(sl[2 * m + j], k), XTh[:, k, h * 512:h * 512 + 512],
                               XTl[:, k, h * 512:h * 512 + 512], k == 0, k == KT - 1)
                mm.then_inc(g(name), 1)
                if last and (i, j) == (2, 0):
                    products(range(4))
        if last and L == 0:
            pe.wait_ge(*g("affine", KT))
        products(range(4, NT) if last else range(NT))

    def ffn_silu(act, L, c, i):
        g = gf[L]
        act.wait_ge(*g("gate", c * 4 + i + 1))
        act.wait_ge(*g("gated", c * 4 + i - 2 + 1 + 2))
        nc.scalar.activation(silu[:, i % 2, :], bank(2 * (i % 2)), ACT.Silu).then_inc(g("silu"), 1)

    def ffn_high(act, L, c, i):
        g = gf[L]
        h, m = i // 2, i % 2
        act.wait_ge(*g("gated", c * 4 + i + 1 + 2))
        nc.scalar.activation(hidh[:, m, h * 512:(h + 1) * 512], hid[:, i % 2, :], ACT.Copy).then_inc(g("hid_high"), 1)

    def ffn_gated(dve, L, c, i):
        g = gf[L]
        dve.wait_ge(*g("silu", c * 4 + i + 1))
        dve.wait_ge(*g("up", c * 4 + i + 1))
        dve.wait_ge(*g("hid_low", c * 4 + i - 2 + 1 + 2))
        nc.vector.tensor_tensor(hid[:, i % 2, :], silu[:, i % 2, :], bank(2 * (i % 2) + 1),
                                ALU.mult).then_inc(g("gated"), 1)

    def ffn_low(dve, L, c, i):
        g = gf[L]
        h, m = i // 2, i % 2
        dve.wait_ge(*g("hid_high", c * 4 + i + 1))
        nc.vector.tensor_tensor(hidl[:, m, h * 512:(h + 1) * 512], hid[:, i % 2, :],
                                hidh[:, m, h * 512:(h + 1) * 512].bitcast(F32),
                                ALU.subtract).then_inc(g("hid_low"), 1)

    def ffn_first(row, one, two, rest=lambda i: None):
        for j in range(KT, 2 * KT):
            row(j)
        for i in range(4):
            one(i)
            two(i)
            rest(i)

    gvp, gup, gsg = Names("vproj"), Names("uproj"), Names("sgu")

    def wide_pe(pe, g, u, n):
        j, t = n // NT, n % NT
        if t == 0:
            pe.wait_ge(split_done, u + 2 * j + 2)
        if n >= 4:
            pe.wait_ge(*g("gelu", n - 3))
        elif g is gup:
            pe.wait_ge(*gvp("gelu", 3 * NT - 3 + n))
        s0 = slot_of(u + 2 * j)
        dst = bank(n % 4, M).rearrange("p (a c) -> p a c", c=P)
        for k in range(KT):
            mm = three(dst, XTh[:, k, t * P:(t + 1) * P], XTl[:, k, t * P:(t + 1) * P],
                       Wh[:, s0:s0 + 2, k * P:(k + 1) * P], Wl[:, s0:s0 + 2, k * P:(k + 1) * P],
                       k == 0, k == KT - 1)
        mm.then_inc(g("product"), 1)

    def channels(n):
        return V[:, n % NT, (n // NT) * M:(n // NT + 1) * M]

    MIX_AT = {3: (0, 1, 2, 3), 4: (4, 5), 5: (6, 7), 6: (8, 9), 7: (10, 11)}

    def turn_ws(pe):
        pe.wait_ge(*gsg("lower", 1))
        for i in range(NG):
            mm = nc.tensor.transpose(bank(4 + i // 4, P, (i % 4) * P), wsraw[:, i, :], ident[:, :])
        mm.then_inc(gsg("ws_turned"), 1)

    def sgu_pe(pe):
        for n in range(3 * NT):
            wide_pe(pe, gvp, U_V, n)
            if n == 8:
                turn_ws(pe)
        for n in range(3 * NT):
            wide_pe(pe, gup, U_U, n)
            if n in MIX_AT:
                pe.wait_ge(*gsg("ws_low", 1))
            for i in MIX_AT.get(n, ()):
                pe.wait_ge(*gsg("v_low", i + 1))
                if i >= 4:
                    pe.wait_ge(*gsg("gate", i - 3))
                three(bank(4 + i % 4), WSh[:, i, :], WSl[:, i, :],
                      VSh[:, i % 2, :, :].rearrange("p a b -> p (a b)"),
                      VSl[:, i % 2, :, :].rearrange("p a b -> p (a b)"), True, True).then_inc(gsg("spatial"), 1)
            t = n - 2 * NT - 1
            if t >= 0:
                sgu_turn(pe, t)
        sgu_turn(pe, NT - 1)

    def sgu_turn(pe, t):
        pe.wait_ge(*gsg("gate", NG))
        pe.wait_ge(*gup("gated", 2 * NT + t + 1))
        turn_pe(pe, gup, t, V[:, t, :], DIL_W // P, 4)

    def sgu_act(act):
        act.wait_ge(sem("mem_mixed"), 8 * NMP + 1)
        act.dma_start(wsraw[:, :, :], a["sgu_w_s"][0].rearrange("g t s -> t g s")).then_inc(gsg("ws_landed"), 16)
        with nc.allow_non_contiguous_dma(reason="1536 biases, once"):
            act.dma_start(bst[:, :], a["sgu_b_s"][0].rearrange("g t -> t g")).then_inc(gsg("bs_landed"), 16)

        for n in range(3 * NT):
            act.wait_ge(*gvp("product", n + 1))
            nc.scalar.activation(channels(n), bank(n % 4, M), ACT.Gelu_apprx_tanh).then_inc(gvp("gelu"), 1)
            if n == 9:
                act.wait_ge(*gsg("ws_turned", 1))
                nc.scalar.activation(WSh[:, :, :], ps[:, 2048:2048 + NG * P].rearrange("p (g t) -> p g t", t=P),
                                     ACT.Copy).then_inc(gsg("ws_high"), 1)
                load_gb(act, gsg, a["sgu_ln_g"][0], a["sgu_ln_b"][0], sgb)
            if n >= 2 * NT and n % 4 == 3:
                t0 = n % NT - 3
                act.wait_ge(*gsg("stats", t0 + 4))
                nc.scalar.activation(rstd[:, t0:t0 + 4], mv[:, t0:t0 + 4, 1], ACT.Sqrt,
                                     bias=eps[:, 0:1]).then_inc(gsg("root"), 1)

        def gelu(n):
            act.wait_ge(*gup("product", n + 1))
            if n >= 2:
                act.wait_ge(*gup("gated", n - 1))
            nc.scalar.activation(ub[:, n % 2, :], bank(n % 4, M), ACT.Gelu_apprx_tanh).then_inc(gup("gelu"), 1)

        gelu(0)
        gelu(1)
        for n in sorted(MIX_AT):
            for i in MIX_AT[n]:
                if i == 0:
                    act.wait_ge(*gsg("shifted", NT))
                if i >= 2:
                    act.wait_ge(*gsg("spatial", i - 1))
                nc.scalar.activation(VSh[:, i % 2, :, :], V[:, :, i * HD:(i + 1) * HD], ACT.Copy
                                     ).then_inc(gsg("v_high"), 1)
            gelu(n - 1)
        act.wait_ge(*gsg("spatial", NG))
        load_gb(act, go[1], a["ln_mix_g"][1], a["ln_mix_b"][1], gb)

        def turn(t):
            ts = slice(t * P, (t + 1) * P)
            turn_act(act, gup, t, DIL_W // P, 4)
            nc.scalar.activation(XTh[:, 6:8, ts], MO[:, :, ts], ACT.Copy).then_inc(gup("mo_high"), 1)

        for n in range(7, 3 * NT):
            gelu(n)
            if n >= 2 * NT + 2:
                turn(n - 2 * NT - 2)
        turn(NT - 2)
        turn(NT - 1)

    def sgu_dve(dve):
        for n in range(3 * NT):
            j, t = n // NT, n % NT
            dve.wait_ge(*gvp("gelu", n + 1))
            nc.vector.bn_stats(st[:, t, j, :], channels(n)).then_inc(gsg("partial"), 1)
            if n == 10:
                dve.wait_ge(*gsg("ws_high", 1))
                nc.vector.tensor_tensor(WSl[:, :, :], ps[:, 2048:2048 + NG * P].rearrange("p (g t) -> p g t", t=P),
                                        WSh[:, :, :].bitcast(F32), ALU.subtract).then_inc(gsg("ws_low"), 1)
            if j == 2:
                dve.wait_ge(*gsg("partial", n + 1))
                nc.vector.bn_aggr(mv[:, t, :], st[:, t, :, :].rearrange("p a b -> p (a b)")).then_inc(gsg("stats"), 1)
                if t % 4 == 3:
                    t0 = t - 3
                    dve.wait_ge(*gsg("root", t // 4 + 1))
                    nc.vector.reciprocal(rstd[:, t0:t0 + 4], rstd[:, t0:t0 + 4]).then_inc(gsg("rstd"), 1)
                    dve.wait_ge(*gsg("rstd", t // 4 + 1))
                    dve.wait_ge(*gsg("gb_landed", 32))
                    for q in range(t0, t0 + 4):
                        nc.vector.tensor_scalar(V[:, q, :], V[:, q, :], mv[:, q, 0:1], rstd[:, q:q + 1], ALU.subtract,
                                                ALU.mult).then_inc(gsg("normed"), 1)
                        dve.wait_ge(*gsg("normed", q + 1))
                        nc.vector.tensor_tensor(V[:, q, :], V[:, q, :], sgb[:, 0, :], ALU.mult).then_inc(gsg("gained"), 1)
        dve.wait_ge(*gsg("bs_landed", 16))

        def gate(i):
            dve.wait_ge(*gsg("spatial", i + 1))
            nc.vector.tensor_scalar(V[:, :, i * HD:(i + 1) * HD], bank(4 + i % 4).rearrange("p (t c) -> p t c", c=HD),
                                    bst[:, i:i + 1], None, ALU.add).then_inc(gsg("gate"), 1)

        def gated(n):
            dve.wait_ge(*gup("gelu", n + 1))
            dve.wait_ge(*gsg("gate", 4 * (n // NT) + 4))
            nc.vector.tensor_tensor(channels(n), channels(n), ub[:, n % 2, :], ALU.mult).then_inc(gup("gated"), 1)

        for n in sorted(MIX_AT):
            for i in MIX_AT[n]:
                dve.wait_ge(*gsg("v_high", i + 1))
                nc.vector.tensor_tensor(VSl[:, i % 2, :, :], V[:, :, i * HD:(i + 1) * HD],
                                        VSh[:, i % 2, :, :].bitcast(F32), ALU.subtract).then_inc(gsg("v_low"), 1)
                if i != MIX_AT[n][0]:
                    gate(i - 1)
            gate(MIX_AT[n][-1])
            if n == 3:
                gated(0)
            gated(n - 2)

        def turn(t):
            ts = slice(t * P, (t + 1) * P)
            turn_dve(dve, gup, t, DIL_W // P, 4)
            dve.wait_ge(*gup("mo_high", t + 1))
            nc.vector.tensor_tensor(XTl[:, 6:8, ts], MO[:, :, ts], XTh[:, 6:8, ts].bitcast(F32),
                                    ALU.subtract).then_inc(gup("mo_low"), 1)

        for n in range(6, 3 * NT):
            gated(n)
            if n >= 2 * NT + 2:
                turn(n - 2 * NT - 2)
        turn(NT - 2)
        turn(NT - 1)

    def sgu_start(pool):
        pool.wait_ge(*gsg("ws_landed", 16))
        nc.gpsimd.affine_select(out=wsraw[:, :, :], in_=wsraw[:, :, :], compare_op=ALU.is_ge, fill=0.0, base=0,
                                pattern=[[0, NG], [-1, P]], channel_multiplier=1).then_inc(gsg("lower"), 1)

    def sgu_pool(pool):
        for t in range(NT):
            pool.wait_ge(*gsg("gained", t + 1))
            nc.gpsimd.tensor_tensor(V[:, t, :], V[:, t, :], sgb[:, 1, :], ALU.add).then_inc(gsg("shifted"), 1)

    DILSL = [0, 1, 2]
    X_FROM = [0, 1, 2, 4, 6, 8]
    X_PARTS = len(X_FROM) - 1
    MIX_ORDER = [0, 1, 2, 3, 4, 6, 7, 5]
    block = nc.Block()
    block.__enter__()

    @block.sync
    def _(sp):
        w = [a["a_w_in"][0], a["b_w_in"][0]]
        mem_q = [3 * DIL_W, 2 * DIL_W]

        def mem_units(L):
            for p in range(NMP):
                u = U_MEM[L] + 3 * p
                load(sp, u, cols(w[L], mem_q[L] + p * P))
                load(sp, u + 1, cols(a["w_mem_kv"][L], p * P))
                load(sp, u + 2, cols(a["w_mem_kv"][L], MEM_W + p * P))

        def out_units(L):
            for k in range(KT):
                if L == 0 and k == 4:
                    for i in range(4):
                        if i == 0:
                            sp.wait_ge(sem("dil_scores"), 16 * NDP)
                        if i == 2:
                            sp.wait_ge(sem("dil_mixed"), 4 * NDP + 1)
                        sp.dma_start(XR[:, 2 * i:2 * i + 2, :],
                                     a["x"][0, 256 * i:256 * i + 256, :].rearrange("(t p) d -> p t d", p=P)
                                     ).then_inc(sem(f"x_again{i}"), 16)
                load(sp, U_OUT[L] + k, a["w_out"][L][k * P:(k + 1) * P, :])

        def ffn_units(L):
            with sp.Fori(0, NCH) as c:
                u = U_FFN[L] + c * 6
                for m in range(2):
                    load(sp, u + 2 * m, cols(a["w_gate"][L], c * 256 + m * P))
                    load(sp, u + 2 * m + 1, cols(a["w_up"][L], c * 256 + m * P))
                for k in range(2):
                    load(sp, u + 4 + k, a["w_down"][L][bass.ds(c * 256 + k * P, P), :])

        mem_units(0)
        for p in range(NDP):
            for j in range(3):
                load(sp, U_DIL + 3 * p + j, cols(w[0], j * DIL_W + p * P))
                if j == 1:
                    for hd in range(2):
                        if p == 0:
                            sp.wait_ge(sem("mem_mixed"), 4 * NMP + 1)
                        else:
                            sp.wait_ge(sem("dil_logits"), 16 * (p - 1) + 14 + 2 * hd)
                        sp.dma_start(DilBuf.B[:, hd, :], a["c_bias"][2 * p + hd]
                                     ).then_inc(sem(f"dil_bias_landed{hd}"), 16)
        out_units(0)
        ffn_units(0)
        mem_units(1)
        for j in range(6):
            load(sp, U_V + j, cols(w[1], DIL_W + j * P))
        for j in range(6):
            load(sp, U_U + j, cols(w[1], j * P))
        out_units(1)
        ffn_units(1)
        for t in range(NT):
            sp.wait_ge(*shifted(gf[1], t))
            sp.dma_start(out[0, t * P:(t + 1) * P, :], XR[:, t, :]).then_inc(sem("stored"), 16)
        sp.wait_ge(sem("stored"), 16 * NT)

    @block.gpsimd
    def _(pool):
        nc.gpsimd.memset(zcol[:, :], 0.0).then_inc(sem("zcol_set"), 1)
        pool.wait_ge(sem("zcol_set"), 1)
        def mix_pool(pool, i):
            if i == 0:
                pool.wait_ge(sem("dil_v_proj"), 2 * NDP)
                pool.wait_ge(sem("dil_mixed"), 4 * (NDP - 1) + 1)
            j = MIX_ORDER[i]
            src = mixT[:, j, :] if j < NDP else MO[:, j - NDP, :]
            nc.gpsimd.tensor_tensor(XTh[:, j, :], src, zcol[:, 0:1].to_broadcast([P, S]), ALU.add
                                    ).then_inc(sem("mix_high"), 1)
            pool.wait_ge(sem("mix_high"), i + 1)
            nc.gpsimd.tensor_tensor(XTl[:, j, :], src, XTh[:, j, :].bitcast(F32), ALU.subtract
                                    ).then_inc(sem("mix_low"), 1)

        attention_over = (sem("dil_mixed"), 4 * NDP + 1)
        for u in range(U_FFN[0]):
            if u == U_OUT[0] + 3:
                for i in range(KT - 1):
                    mix_pool(pool, i)
            split(pool, u, attention_over if U_OUT[0] + 3 <= u < U_OUT[0] + 6 else None)

        def ffn_units(L):
            for j in range(4):
                split(pool, U_FFN[L] + j)
            row_pool(pool, go[L], range(2 * KT))
            for j in range(4, 6):
                split(pool, U_FFN[L] + j)
            norm_pool(pool, go[L], range(0, NT, 2))
            with pool.Fori(1, NCH) as c:
                for j in range(6):
                    split(pool, U_FFN[L] + c * 6 + j, used(U_FFN[L] + j, c - 1), (U_FFN[L] + j) % RS,
                          U_FFN[L] // 2 + c * 3 + j // 2 + 1, slot_of(U_FFN[L] + j))

        ffn_units(0)
        row_pool(pool, gf[0], range(KT))
        for j in range(3):
            split(pool, U_MEM[1] + j)
        row_pool(pool, gf[0], range(KT, 2 * KT))
        for j in range(3, 5):
            split(pool, U_MEM[1] + j)
        norm_pool(pool, gf[0], range(6))
        split(pool, U_MEM[1] + 5)
        norm_pool(pool, gf[0], range(6, NT), 6)
        for u in range(U_MEM[1] + 6, U_U):
            split(pool, u, (sem("mem_mixed"), 8 * NMP + 1) if U_V + 3 <= u < U_V + 6 else None)
            if u == U_V + 1:
                sgu_start(pool)
        for u in range(U_U, U_U + 4):
            split(pool, u)
        sgu_pool(pool)
        for u in range(U_U + 4, U_FFN[1]):
            split(pool, u)
        ffn_units(1)
        norm_pool(pool, gf[1], range(NT), last=True)

    @block.tensor
    def _(pe):
        pe.wait_ge(sem("const_landed"), 16)
        for t in range(NT):
            if t in X_FROM:
                pe.wait_ge(sem(f"x_landed{X_FROM.index(t)}"), 16)
            turn_pe(pe, gi, t, XR[:, t, :], bb=4 * (t >= 4))
            if t >= 4:
                if t == 4:
                    pe.wait_ge(*gi("xt_low", 4))
                    pe.wait_ge(split_done, U_MEM[0] + 1)
                for k in (2 * (t - 4), 2 * (t - 4) + 1):
                    mm = three(bank(0), *wtile(slot_of(U_MEM[0]), k), XTh[:, k, 0:512], XTl[:, k, 0:512],
                               k == 0, k == KT - 1)
                if t == NT - 1:
                    mm.then_inc(sem("mem_qk_proj"), 1)
        for t in range(2):
            pe.wait_ge(*gi("xt_low", NT - 1 + t))
            pe.wait_ge(sem("mem_landed0"), 16)
            turn_pe(pe, gm[0], t, memraw[:, t, :], bb=4)
        for L in range(2):
            def slots(p):
                return [slot_of(U_MEM[L] + 3 * p + j) for j in range(3)]

            def mem_qk(p):
                return fills(lambda j: qk_pe(pe, "mem", j, U_MEM[L] + 3 * p, slots(p)), "mem")

            def dil_qk(p):
                return fills(lambda j: qk_pe(pe, "dil", j, U_DIL + p * 3, DILSL), "dil")

            if L == 0:
                pe.wait_ge(*gi("xt_low", NT))
                pe.wait_ge(*gm[0]("xt_low", 2))
                for f in mem_qk(0)[1:]:
                    f()
            else:
                q0, k_, q1 = mem_qk(0)
                pe.wait_ge(*gf[0]("xt_low", KT))
                q0()
                pe.wait_ge(sem("mem_landed1"), 16)
                turn_pe(pe, gm[1], 0, memraw[:, 0, :], bb=2)
                pe.wait_ge(*gf[0]("added", 16 * NCH + gf[0].credit))
                turn_pe(pe, gm[1], 1, memraw[:, 1, :], bb=2)
                for j in range(KT, 2 * KT):
                    if j == KT + 2:
                        pe.wait_ge(*gm[1]("xt_low", 2))
                    row_turn(pe, gf[0], j, NCH - 1)
                k_()
                pe.wait_ge(*gf[0]("xt_low", 2 * KT))
                q1()
            for p in range(NMP):
                pair_pe(pe, "mem", NMP * L + p, U_MEM[L] + 3 * p, slots(p),
                        mem_qk(p + 1) if p < NMP - 1 else dil_qk(0) if L == 0 else [])
            if L == 0:
                with pe.Fori(0, NDP - 1) as p:
                    pair_pe(pe, "dil", p, p * 3 + U_DIL, DILSL, dil_qk(p + 1))
                pair_pe(pe, "dil", NDP - 1, U_DIL + 3 * (NDP - 1), DILSL, [])
                pe.wait_ge(sem("dil_mixed"), 4 * NDP + 1)
            else:
                pe.wait_ge(sem("mem_mixed"), 8 * NMP + 1)
                sgu_pe(pe)
                pe.wait_ge(*gup("xt_low", NT))

            for c in range(KT // 2):
                def ready(t):
                    if L == 0 and t == 0:
                        if c == 2:
                            pe.wait_ge(sem("last_low"), 1)
                        pe.wait_ge(sem("mix_low"), min(2 * c + 2, KT - 1) if c != 2 else 5)
                    if L == 1 and c == 0:
                        pe.wait_ge(*gup("mo_low", t + 1))
                u = U_OUT[L] + 2 * c
                acc_pe(pe, go[L], c, u,
                       lambda k, t: (XTh[:, 2 * c + k, t * P:(t + 1) * P], XTl[:, 2 * c + k, t * P:(t + 1) * P]),
                       [slot_of(u), slot_of(u + 1)], ready, after=norm_pe_after(pe, go[L], c) if c == 3 else None)
            ffn_pe(pe, L, 0, True, False)
            with pe.Fori(1, NCH - 1) as c:
                ffn_pe(pe, L, c, False, False)
            ffn_pe(pe, L, NCH - 1, False, True)

    @block.scalar
    def _(act):
        act.dma_start(ident[:, :], a["c_ident"]).then_inc(sem("const_landed"), 16)
        for i in range(X_PARTS):
            act.dma_start(XR[:, X_FROM[i]:X_FROM[i + 1], :],
                          a["x"][0, P * X_FROM[i]:P * X_FROM[i + 1], :].rearrange("(t p) d -> p t d", p=P)
                          ).then_inc(sem(f"x_landed{i}"), 16)
        mem = a["mem"][0].rearrange("(t p) d -> p t d", p=P)
        act.dma_start(memraw[:, :, :], mem).then_inc(sem("mem_landed0"), 16)
        for t in range(NT):
            turn_act(act, gi, t, bb=4 * (t >= 4))
        for t in range(2):
            turn_act(act, gm[0], t, bb=4, high=memTh)
        for L in range(2):
            def mem_qk(p):
                return fills(lambda j: qk_act(act, "mem", NMP * L + p, j), "mem")

            def dil_qk(p):
                return fills(lambda j: qk_act(act, "dil", p, j), "dil")

            if L == 0:
                for f in mem_qk(0):
                    f()
            for p in range(NMP):
                pair_act(act, "mem", NMP * L + p, mem_qk(p + 1) if p < NMP - 1 else dil_qk(0) if L == 0 else [])
            if L == 0:
                with act.Fori(0, NDP - 1) as p:
                    pair_act(act, "dil", p, dil_qk(p + 1))

                pair_act(act, "dil", NDP - 1, [])
                act.wait_ge(sem("dil_mixed"), 4 * NDP + 1)
                nc.scalar.activation(XTh[:, NDP - 1, :], mixT[:, NDP - 1, :], ACT.Copy).then_inc(sem("last_high"), 1)
                load_gb(act, go[0], a["ln_mix_g"][0], a["ln_mix_b"][0], gb)
            else:
                sgu_act(act)
            load_cols(act, go[L], a["ln_mix_g"][L], a["ln_mix_b"][L])
            norm_act(act, go[L], range(NT), UNITS_AT)
            ffn_first(lambda j: row_act(act, go[L], j), lambda i: ffn_silu(act, L, 0, i), lambda i: ffn_high(act, L, 0, i))
            load_cols(act, gf[L], a["ln_ffn_g"][L], a["ln_ffn_b"][L]) if L == 0 else None
            act.wait_ge(*go[L]("shifted", NT // 2))
            act.wait_ge(*go[L]("odd_shifted", NT // 2))
            if L == 0:
                act.wait_ge(sem("mix_low"), KT - 1)
                act.wait_ge(sem("last_low"), 1)
                act.dma_start(memraw[:, :, :], mem).then_inc(sem("mem_landed1"), 16)
            else:
                load_gb(act, gf[1], a["ln_ffn_g"][1], a["ln_ffn_b"][1], gb)
            with act.Fori(1, NCH - 1) as c:
                for i in range(4):
                    ffn_silu(act, L, c, i)
                    ffn_high(act, L, c, i)
            for i in range(4):
                if i == 2:
                    norm_act(act, gf[L], range(4))
                    for j in range(KT if L == 0 else 0):
                        row_act(act, gf[0], j)
                ffn_silu(act, L, NCH - 1, i)
                ffn_high(act, L, NCH - 1, i)

            if L == 0:
                act.wait_ge(*gf[0]("hid_low", 4 * NCH + 2))
                load_row(act, gf[0], a["ln_ffn_g"][0], g_mem[:, 0, :])
                load_row(act, gf[0], a["ln_ffn_b"][0], b_mem[:, 0, :])
            norm_act(act, gf[L], range(4, NT))
            if L == 0:
                q0, k_, q1 = fills(lambda j: qk_act(act, "mem", NMP, j), "mem")
                q0()
                for t in range(2):
                    turn_act(act, gm[1], t, bb=2, high=memTh)
                for j in range(KT, 2 * KT):
                    row_act(act, gf[0], j)
                k_()
                q1()

    @block.vector
    def _(dve):
        def clear_queries(g, bf):
            for q in (bf.Qh, bf.Ql):
                nc.vector.memset(q[HD:P, 0, :].bitcast(F32), 0.0).then_inc(g("cleared"), 1)
                nc.vector.memset(q[0:HD, 1, :].bitcast(F32), 0.0).then_inc(g("cleared"), 1)

        def attention_start(g, bf, times=1, queries=True):
            if queries:
                clear_queries(g, bf)
            for v in (bf.Vh, bf.Vl):
                nc.vector.memset(v[:, :, HD:2 * HD].bitcast(F32), 0.0).then_inc(g("cleared"), 1)
            dve.wait_ge(*g("cleared", 6 * times))
            if times == 1:
                dve.sem_inc(g("mixed"), 1)

        nc.vector.memset(eps[:, :], EPS).then_inc(sem("eps_set"), 1)
        clear_queries(pair_names("mem"), MemBuf)
        for t in range(NT):
            turn_dve(dve, gi, t, bb=4 * (t >= 4))
        def memory_start(L):
            g = pair_names("mem")
            nc.vector.memset(MemBuf.zero[:, :], 0.0).then_inc(g("zeroed"), 1)
            dve.wait_ge(*g("zeroed", L + 1))
            attention_start(g, MemBuf, L + 1, queries=L == 1)

        for t in range(2):
            turn_dve(dve, gm[0], t, bb=4, high=memTh, low=memTl)
        dve.wait_ge(*gm[0]("xt_low", 2))
        memory_start(0)
        for L in range(2):
            def mem_qk(p):
                return fills(lambda j: qk_dve(dve, "mem", NMP * L + p, j), "mem")

            def dil_qk(p):
                return fills(lambda j: qk_dve(dve, "dil", p, j), "dil")

            if L == 0:
                for f in mem_qk(0):
                    f()
            for p in range(NMP):
                def beside(i):
                    if L == 1 and p == 1 and i == 1:
                        dve.wait_ge(*gf[0]("shifted", NT))

                fill = mem_qk(p + 1) if p < NMP - 1 else dil_qk(0) if L == 0 else []
                if L == 0 and p == 0:
                    fill[0] = lambda f=fill[0]: (clear_queries(pair_names("dil"), DilBuf), f())
                    fill[2] = lambda f=fill[2]: (attention_start(pair_names("dil"), DilBuf, queries=False), f())
                pair_dve(dve, "mem", NMP * L + p, mem_dst, fill, beside)
            if L == 0:
                with dve.Fori(0, NDP - 1) as p:
                    pair_dve(dve, "dil", p, dil_dst, dil_qk(p + 1))

                pair_dve(dve, "dil", NDP - 1, dil_dst, [])
                dve.wait_ge(sem("last_high"), 1)
                nc.vector.tensor_tensor(XTl[:, NDP - 1, :], mixT[:, NDP - 1, :], XTh[:, NDP - 1, :].bitcast(F32),
                                        ALU.subtract).then_inc(sem("last_low"), 1)
            else:
                sgu_dve(dve)
            for c in range(KT // 2 - 1):
                for t in range(NT):
                    if L == 0 and c == 0 and t % 2 == 0:
                        dve.wait_ge(sem(f"x_again{t // 2}"), 16)
                    acc_dve(dve, go[L], c, t, ALPHA if c == 0 else None)
            if L == 0:
                dve.sem_inc(gf[L]("gated"), 2)
                dve.sem_inc(gf[L]("hid_low"), 2)
                dve.sem_inc(gf[L]("added"), 4)
            norm_dve(dve, go[L], KT // 2 - 1, range(NT), UNITS_AT)
            ffn_first(lambda j: row_dve(dve, go[L], j), lambda i: ffn_gated(dve, L, 0, i),
                      lambda i: ffn_low(dve, L, 0, i), lambda i: odd_rows_dve(dve, go[L], 2 * i + 1))
            for t in range(NT):
                dve.wait_ge(*go[L]("odd_shifted" if t % 2 else "shifted", t // 2 + 1))
                acc_dve(dve, gf[L], 0, t, ALPHA)
            with dve.Fori(1, NCH - 1) as c:
                for i in range(4):
                    ffn_gated(dve, L, c, i)
                    ffn_low(dve, L, c, i)
                for t in range(NT):
                    acc_dve(dve, gf[L], c, t)
            for i in range(4):
                if i == 2:
                    norm_dve(dve, gf[L], NCH - 1, range(4))
                    if L == 0:
                        for j in range(KT):
                            row_dve(dve, gf[0], j)
                    else:
                        for q in range(4):
                            final_dve(dve, q)
                ffn_gated(dve, L, NCH - 1, i)
                ffn_low(dve, L, NCH - 1, i)

            norm_dve(dve, gf[L], NCH - 1, range(4, NT))
            if L == 1:
                for q in range(4, NT):
                    final_dve(dve, q)
            if L == 0:
                for t in range(2):
                    turn_dve(dve, gm[1], t, bb=2, high=memTh, low=memTl)
                q0, k_, q1 = fills(lambda j: qk_dve(dve, "mem", NMP, j), "mem")
                for j in range(KT, 2 * KT):
                    row_dve(dve, gf[0], j)
                dve.wait_ge(*gf[0]("xt_low", 2 * KT))
                memory_start(1)
                q0()
                k_()
                q1()

    block.__exit__(None, None, None)


_INS = ["x", "mem", "a_w_in", "b_w_in", "sgu_ln_g", "sgu_ln_b", "sgu_w_s", "sgu_b_s", "w_mem_kv", "w_out",
        "ln_mix_g", "ln_mix_b", "w_gate", "w_up", "w_down", "ln_ffn_g", "ln_ffn_b"]


def kernel(**inputs):
    import concourse.bacc as bacc
    from concourse.bass_utils import run_bass_kernel_spmd

    nc = bacc.Bacc("TRN2", target_bir_lowering=False, num_devices=1)
    arrays = {n: np.ascontiguousarray(inputs[n]) for n in _INS}
    arrays.update(zip(("c_bias", "c_ident"), tables()))
    a = {n: nc.dram_tensor(f"in_{n}", v.shape, mybir.dt.from_np(v.dtype), kind="ExternalInput").ap()
         for n, v in arrays.items()}
    out = nc.dram_tensor("out_0", (1, S, D), F32, kind="ExternalOutput").ap()
    build(nc, a, out)
    r = run_bass_kernel_spmd(nc, [{f"in_{n}": v for n, v in arrays.items()}], core_ids=[0])
    return r.results[0]["out_0"]
```
